# Optimizing a Trainium2 kernel written in Bass

```python
import math
import jax, jax.numpy as jnp
from jax import lax
import numpy as np

D_MODEL = 1024
BATCH = 1
SEQ = 512
DEPTH = 2

CONV_WIDTH = 3
A_WIDTH = D_MODEL // 2
A_HEADS = 8
B_WIDTH = D_MODEL // 2
POOL_WINDOWS = (2, 4, 8, 16)
N_POOL_GROUPS = len(POOL_WINDOWS)
POOL_GROUP = B_WIDTH // N_POOL_GROUPS
EVEN_IN = 3 * A_WIDTH + B_WIDTH
HEAD_DIM = 64
N_HEADS = D_MODEL // HEAD_DIM
DILATED_PAIRS = ((128, 1), (512, 4), (2048, 16))
N_REL_BUCKETS = 32
REL_MAX_DISTANCE = 2048
D_FF = 2816
EPS = 1e-6
MASK_VALUE = -1e30
N_EVEN = (DEPTH + 1) // 2
N_ODD = DEPTH // 2

kernel_name = "hybrid_conv_pool_dilated_attn_trunk"

def rmsnorm(x, g):
    x32 = x.astype(jnp.float32)
    y = x32 * lax.rsqrt(jnp.mean(x32 * x32, axis=-1, keepdims=True) + EPS)
    return (y * g.astype(jnp.float32)).astype(x.dtype)

def causal_dwconv3(x, w):
    S = x.shape[1]
    xp = jnp.pad(x, ((0, 0), (CONV_WIDTH - 1, 0), (0, 0)))
    y = xp[:, 0:S] * w[0]
    for i in range(1, CONV_WIDTH):
        y = y + xp[:, i:i + S] * w[i]
    return y

def causal_window_mean(p, k):
    S = p.shape[1]
    cs = jnp.cumsum(p, axis=1)
    cs_prev = jnp.pad(cs, ((0, 0), (k, 0), (0, 0)))[:, :S]
    cnt = jnp.minimum(jnp.arange(1, S + 1), k).astype(jnp.float32)[None, :, None]
    return (cs - cs_prev) / cnt

def t5_causal_bucket(dist):
    max_exact = N_REL_BUCKETS // 2
    d = jnp.maximum(dist, 1).astype(jnp.float32)
    large = max_exact + (jnp.log(d / max_exact) / math.log(REL_MAX_DISTANCE / max_exact)
                         * (N_REL_BUCKETS - max_exact)).astype(jnp.int32)
    large = jnp.minimum(large, N_REL_BUCKETS - 1)
    return jnp.where(dist < max_exact, dist, large)

def conv_pool_mixer(xn, w_in, conv_w, pool_w, pool_scale, w_out):
    B, S, _ = xn.shape
    proj = xn @ w_in
    h, gate_b, gate_c, pin = jnp.split(proj, [A_WIDTH, 2 * A_WIDTH, 3 * A_WIDTH], axis=-1)
    ya = gate_b * causal_dwconv3(gate_c * h, conv_w)
    p32 = pin.astype(jnp.float32).reshape(B, S, N_POOL_GROUPS, POOL_GROUP)
    pooled = jnp.stack([causal_window_mean(p32[:, :, g], k)
                        for g, k in enumerate(POOL_WINDOWS)], axis=2) - p32
    yb = jnp.einsum('bsgc,gcd->bsgd', pooled, pool_w.astype(jnp.float32))
    yb = (yb.reshape(B, S, B_WIDTH) * pool_scale.astype(jnp.float32)).astype(xn.dtype)
    return jnp.concatenate([ya, yb], axis=-1) @ w_out

def dilated_branch(q, k, v, rel_table, window, dil):
    B, S, H, E = q.shape
    n = window // dil
    QB = n
    L = S // dil
    nb = -(-L // QB)
    Lp = nb * QB

    def residues(t):
        return jnp.swapaxes(t.reshape(B, L, dil, H, E), 1, 2)

    qr = jnp.pad(residues(q), ((0, 0), (0, 0), (0, Lp - L), (0, 0), (0, 0)))
    kp = jnp.pad(residues(k), ((0, 0), (0, 0), (n, Lp - L), (0, 0), (0, 0)))
    vp = jnp.pad(residues(v), ((0, 0), (0, 0), (n, Lp - L), (0, 0), (0, 0)))

    def key_blocks(t):
        prev = t[:, :, :Lp].reshape(B, dil, nb, QB, H, E)
        cur = t[:, :, n:].reshape(B, dil, nb, QB, H, E)
        return jnp.concatenate([prev, cur], axis=3)

    qb = qr.reshape(B, dil, nb, QB, H, E)
    kb = key_blocks(kp)
    vb = key_blocks(vp)

    a = jnp.arange(QB)[:, None]
    c = jnp.arange(2 * QB)[None, :]
    rel = a + n - c
    key_pos = jnp.arange(nb)[:, None] * QB - n + jnp.arange(2 * QB)[None, :]
    valid = ((rel >= 0) & (rel <= n))[None] & (key_pos >= 0)[:, None, :]
    bias = rel_table.astype(jnp.float32)[t5_causal_bucket(jnp.clip(rel, 0, n) * dil)]
    bias = jnp.transpose(bias, (2, 0, 1))

    s = jnp.einsum('bdnqhe,bdnkhe->bdnhqk', qb, kb) * (HEAD_DIM ** -0.5) + bias
    s = jnp.where(valid[None, None, :, None], s, MASK_VALUE)
    m = jnp.max(s, axis=-1)
    p = jnp.exp(s - m[..., None])
    den = jnp.sum(p, axis=-1)
    m = jnp.swapaxes(m, 3, 4)
    den = jnp.swapaxes(den, 3, 4)
    o = jnp.einsum('bdnhqk,bdnkhe->bdnqhe', p, vb) / den[..., None]

    def from_blocks(t):
        rest = t.shape[5:]
        t = t.reshape((B, dil, Lp, H) + rest)[:, :, :L]
        return jnp.swapaxes(t, 1, 2).reshape((B, S, H) + rest)

    return from_blocks(o), from_blocks(m), from_blocks(den)

def dilated_attention(xn, w_qkv, g_q, g_k, w_o, rel_table):
    B, S, D = xn.shape
    qkv = (xn @ w_qkv).reshape(B, S, 3, N_HEADS, HEAD_DIM).astype(jnp.float32)
    q = rmsnorm(qkv[:, :, 0], g_q)
    k = rmsnorm(qkv[:, :, 1], g_k)
    v = qkv[:, :, 2]
    outs, maxes, dens = [], [], []
    for window, dil in DILATED_PAIRS:
        o, m, den = dilated_branch(q, k, v, rel_table, window, dil)
        outs.append(o)
        maxes.append(m)
        dens.append(den)
    outs = jnp.stack(outs)
    maxes = jnp.stack(maxes)
    dens = jnp.stack(dens)
    wts = dens * jnp.exp(maxes - jnp.max(maxes, axis=0, keepdims=True))
    o = jnp.sum(wts[..., None] * outs, axis=0) / jnp.sum(wts, axis=0)[..., None]
    return o.reshape(B, S, D).astype(xn.dtype) @ w_o

def conv_glu_ffn(xn, w_up, conv_w, conv_b, w_down):
    u = causal_dwconv3(xn @ w_up, conv_w) + conv_b
    gate, up = jnp.split(u, 2, axis=-1)
    return (jax.nn.silu(gate) * up) @ w_down

def setup_inputs(seed: int = 0) -> dict:
    key = jax.random.key(seed)
    ks = jax.random.split(key, 20)
    f32 = jnp.float32

    def nrm(k, shape, scale):
        return jax.random.normal(k, shape, f32) * scale

    return {
        "x": nrm(ks[0], (BATCH, SEQ, D_MODEL), 1.0),
        "rel_bias": nrm(ks[1], (N_REL_BUCKETS, N_HEADS), 0.5),
        "even_norm": 1.0 + nrm(ks[2], (N_EVEN, D_MODEL), 0.02),
        "even_w_in": nrm(ks[3], (N_EVEN, D_MODEL, EVEN_IN), D_MODEL ** -0.5),
        "even_conv_w": nrm(ks[4], (N_EVEN, CONV_WIDTH, A_WIDTH), CONV_WIDTH ** -0.5),
        "even_pool_w": nrm(ks[5], (N_EVEN, N_POOL_GROUPS, POOL_GROUP, POOL_GROUP), POOL_GROUP ** -0.5),
        "even_pool_scale": 1.0 + nrm(ks[6], (N_EVEN, B_WIDTH), 0.02),
        "even_w_out": nrm(ks[7], (N_EVEN, D_MODEL, D_MODEL), D_MODEL ** -0.5),
        "odd_norm": 1.0 + nrm(ks[8], (N_ODD, D_MODEL), 0.02),
        "odd_w_qkv": nrm(ks[9], (N_ODD, D_MODEL, 3 * D_MODEL), D_MODEL ** -0.5),
        "odd_q_norm": 1.0 + nrm(ks[10], (N_ODD, HEAD_DIM), 0.02),
        "odd_k_norm": 1.0 + nrm(ks[11], (N_ODD, HEAD_DIM), 0.02),
        "odd_w_o": nrm(ks[12], (N_ODD, D_MODEL, D_MODEL), D_MODEL ** -0.5),
        "ffn_norm": 1.0 + nrm(ks[13], (DEPTH, D_MODEL), 0.02),
        "ffn_w_up": nrm(ks[14], (DEPTH, D_MODEL, 2 * D_FF), D_MODEL ** -0.5),
        "ffn_conv_w": nrm(ks[15], (DEPTH, CONV_WIDTH, 2 * D_FF), CONV_WIDTH ** -0.5),
        "ffn_conv_b": nrm(ks[16], (DEPTH, 2 * D_FF), 0.02),
        "ffn_w_down": nrm(ks[17], (DEPTH, D_FF, D_MODEL), D_FF ** -0.5),
    }

def reference(x, rel_bias, even_norm, even_w_in, even_conv_w, even_pool_w, even_pool_scale,
              even_w_out, odd_norm, odd_w_qkv, odd_q_norm, odd_k_norm, odd_w_o,
              ffn_norm, ffn_w_up, ffn_conv_w, ffn_conv_b, ffn_w_down):
    for layer in range(DEPTH):
        i = layer // 2
        if layer % 2 == 0:
            x = x + conv_pool_mixer(rmsnorm(x, even_norm[i]), even_w_in[i], even_conv_w[i],
                                    even_pool_w[i], even_pool_scale[i], even_w_out[i])
        else:
            x = x + dilated_attention(rmsnorm(x, odd_norm[i]), odd_w_qkv[i], odd_q_norm[i],
                                      odd_k_norm[i], odd_w_o[i], rel_bias)
        x = x + conv_glu_ffn(rmsnorm(x, ffn_norm[layer]), ffn_w_up[layer], ffn_conv_w[layer],
                             ffn_conv_b[layer], ffn_w_down[layer])
    return x


_drawn_inputs = setup_inputs


def setup_inputs(seed=0):
    import zlib

    import numpy as np

    out = dict(_drawn_inputs(seed))
    spreads = {}
    factors = {'even_pool_scale': 5.192,
     'odd_norm': 8.0,
     'odd_q_norm': 8.0,
     'odd_k_norm': 8.0,
     'ffn_norm': 3.309,
     'ffn_conv_b': 3.44}
    for name, (base, spread) in spreads.items():
        noise = np.random.default_rng([zlib.crc32(name.encode()), seed]).standard_normal(out[name].shape)
        drawn = base * np.exp(spread * noise) if base else spread * noise
        out[name] = __import__('jax').numpy.asarray(drawn.astype(out[name].dtype))
    for name, factor in factors.items():
        out[name] = (out[name] * factor).astype(out[name].dtype)
    return out
```

```python
from contextlib import ExitStack
import math

import numpy as np

import concourse.bass as bass
from concourse import mybir

F32 = mybir.dt.float32
F32R = mybir.dt.float32r
I32 = mybir.dt.int32
ALU = mybir.AluOpType
ACT = mybir.ActivationFunctionType

P = 128
SEQ = 512
D = 1024
KT = D // P
TB = SEQ // P
D_FF = 2816
FT = D_FF // P
A_WIDTH = D // 2
GROUPS = A_WIDTH // P
POOL_WINDOWS = (2, 4, 8, 16)
PAD = max(POOL_WINDOWS)
TAPS = 3
HEAD = 64
PAIRS = D // (2 * HEAD)
DILATED = ((128, 1), (512, 4), (2048, 16))
BUCKETS = 32
REL_MAX = 2048
EPS = 1e-6
MASKED = -1e30
NVEC = SEQ + 2 * P

RING = 4
SLOT = KT * P
DOWN_SPLIT = (6, 6, 5, 5)
assert sum(DOWN_SPLIT) == FT

U_IN = 0
U_OUT = U_IN + 4 * GROUPS
U_UP0 = U_OUT + KT
U_DOWN0 = U_UP0 + 2 * FT
U_QKV = U_DOWN0 + 4 * KT
U_WO = U_QKV + 4 * PAIRS
U_UP1 = U_WO + KT
U_DOWN1 = U_UP1 + 2 * FT
UNITS = U_DOWN1 + 4 * KT
assert all(u % RING == 0 for u in (U_OUT, U_UP0, U_DOWN0, U_QKV, U_WO, U_UP1, U_DOWN1, UNITS))

C_GAIN = 0
C_QK = C_GAIN + 4 * KT
C_CONVA = C_QK + 2
C_PSCALE = C_CONVA + TAPS * GROUPS
C_FFN = C_PSCALE + GROUPS
C_ONE = C_FFN + 2 * FT * 8
C_HEAD = C_ONE + 1
C_INV = C_HEAD + 2
C_IDENT = C_INV + GROUPS * PAD
NPAR = C_IDENT + P

MIX = 0
POOLED = 8
POOLW = 12
QT = 8
KTILE = 10
VT = 12
PT = 15
VW = 3 * HEAD

SCORES = sum(P * (b + 1) for b in range(TB))
PACK = [(3, 0, 512), (2, 512, 384), (0, 896, 128), (1, 1024, 256)]
MAGIC = float(0x5F3759DF)


def relative_bucket(dist):
    exact = BUCKETS // 2
    if dist < exact:
        return dist
    large = exact + int(math.log(dist / exact) / math.log(REL_MAX / exact) * (BUCKETS - exact))
    return min(large, BUCKETS - 1)


def shape_constants():
    onehot = np.zeros((BUCKETS, NVEC), np.float32)
    count = np.full((2 * PAIRS, NVEC), MASKED, np.float32)
    for y in range(P - 1, P - 1 + SEQ):
        dist = y - (P - 1)
        n = sum(dist % dil == 0 and dist <= window for window, dil in DILATED)
        if n:
            onehot[relative_bucket(dist), y] = 1.0
            count[:, y] = math.log(n)
    return onehot, count


class Steps:

    def __init__(self, eng, sem):
        self.eng, self.sem, self.base, self.n = eng, sem, 0, 0

    def link(self, instruction):
        self.n += 1
        instruction.then_inc(self.sem, 1)
        self.eng.wait_ge(self.sem, self.base + self.n)

    def loop(self, i, first, per):
        self.before = self.base + self.n
        self.base, self.n, self.per = self.before + (i - first) * per, 0, per

    def end(self, rounds):
        assert self.n == self.per, (self.n, self.per)
        self.base, self.n = self.before + rounds * self.per, 0


def trunk(nc, xt, params, onehot, count, rel, poolw, w_in, w_out, w_up, w_down, w_qkv, w_o, out):
    bias_rows = nc.dram_tensor("bias_rows", [2 * PAIRS, NVEC], F32, kind="Internal").ap()
    with ExitStack() as ctx:
        def sb(name, shape, dt=F32):
            return ctx.enter_context(nc.sbuf_tensor(name, shape, dt))

        def sem(name):
            return ctx.enter_context(nc.semaphore(name))

        x = sb("x", [P, KT, SEQ])
        xh = sb("xh", [P, KT, SEQ], F32R)
        xl = sb("xl", [P, KT, SEQ], F32R)
        bh = sb("bh", [P, FT, SEQ], F32R)
        bl = sb("bl", [P, FT, SEQ], F32R)
        raw = [sb(f"raw{s}", [P, SLOT]) for s in range(RING)]
        wh = [sb(f"wh{s}", [P, SLOT], F32R) for s in range(RING)]
        wl = [sb(f"wl{s}", [P, SLOT], F32R) for s in range(RING)]
        par = sb("par", [P, NPAR])
        rstd = sb("rstd", [P, SEQ])
        acc = sb("acc", [P, SEQ])
        sq = sb("sq", [P, SEQ])
        small = sb("small", [P, 5, 16])
        guess = sb("guess", [P, 16], I32)
        epsv = sb("epsv", [P, TB])
        gqs = sb("gqs", [P, 1])
        work = sb("work", [P, 6200])

        def tiles(sizes):
            at, views = 0, []
            for n in sizes:
                views.append(work[:, at:at + n])
                at += n
            assert at <= 6200
            return views

        hs, zc, cv, ya, pin, pa, pb, pooled, cs, poolraw = tiles(
            [SEQ, SEQ + 2, SEQ, SEQ, SEQ + PAD, SEQ + PAD, SEQ + PAD, SEQ, SEQ, GROUPS * P])
        zg0, zu0, zg1, zu1, ug, uu0, uu1, sg, hf = tiles([SEQ + 2] * 4 + [SEQ] * 5)
        zg, zu, uu = [zg0, zg1], [zu0, zu1], [uu0, uu1]
        sc, t0, t1, vf, sqq, sqk, qg, kg, rq, rk = tiles([SCORES] + [SEQ] * 9)
        toep = [t0, t1]
        oh_sb, cnt_sb, rel_sb = tiles([NVEC, NVEC, 2 * PAIRS])
        bv_sb = sb("bv_sb", [P, NVEC])
        sq_first = [sq[:], pooled, cs, pin[:, 0:SEQ]]
        nmax = sb("nmax", [P, TB])
        gate = sb("gate", [P, 1])
        den = sb("den", [P, TB])
        rden = sb("rden", [P, TB])

        bank = [ctx.enter_context(nc.psum_tensor(f"bank{b}", [P, SEQ], F32)) for b in range(4)]
        spt = ctx.enter_context(nc.psum_tensor("spt", [P, 3 * SEQ], F32))
        obank = ctx.enter_context(nc.psum_tensor("obank", [P, SEQ], F32))
        rbank = [spt[:, 0:SEQ], spt[:, SEQ:2 * SEQ]]
        nbank = spt[:, 2 * SEQ:3 * SEQ]
        mbank = bank[3]

        s_par = sem("s_par")
        s_xin = [sem(f"s_xin{n}") for n in range(4)]
        s_pool = sem("s_pool")
        s_setup = sem("s_setup")
        s_bvmm = sem("s_bvmm")
        s_bv = sem("s_bv")
        s_rows = sem("s_rows")
        s_raw = [sem(f"s_raw{s}") for s in range(RING)]
        s_hi = sem("s_hi")
        s_lo = sem("s_lo")
        s_unit = sem("s_unit")
        s_x = sem("s_x")
        s_xh = sem("s_xh")
        s_xl = sem("s_xl")
        s_sq = sem("s_sq")
        s_acc = sem("s_acc")
        s_ms = sem("s_ms")
        s_rn = sem("s_rn")
        s_bc = sem("s_bc")
        s_rstd = sem("s_rstd")
        s_small = sem("s_small")
        s_inev = sem("s_inev")
        s_zc = sem("s_zc")
        s_cv = sem("s_cv")
        s_ya = sem("s_ya")
        s_yah = sem("s_yah")
        s_yal = sem("s_yal")
        s_pd = sem("s_pd")
        s_pdh = sem("s_pdh")
        s_pdl = sem("s_pdl")
        s_pwh = sem("s_pwh")
        s_pwl = sem("s_pwl")
        s_yb = sem("s_yb")
        s_ybh = sem("s_ybh")
        s_ybl = sem("s_ybl")
        s_z = sem("s_z")
        s_id = sem("s_id")
        s_t1 = sem("s_t1")
        s_t0 = sem("s_t0")
        s_silu = sem("s_silu")
        s_h = sem("s_h")
        s_hh = sem("s_hh")
        s_hl = sem("s_hl")
        s_t = [sem("s_ta"), sem("s_tb")]
        s_vf = sem("s_vf")
        s_vt = sem("s_vt")
        s_vh = sem("s_vh")
        s_vl = sem("s_vl")
        s_qs = sem("s_qs")
        s_st = sem("s_st")
        s_r = sem("s_r")
        s_rb = sem("s_rb")
        s_qn = sem("s_qn")
        s_qh = sem("s_qh")
        s_ql = sem("s_ql")
        s_s = sem("s_s")
        s_neg = sem("s_neg")
        s_e = sem("s_e")
        s_p = sem("s_p")
        s_pt = sem("s_pt")
        s_pth = sem("s_pth")
        s_ptl = sem("s_ptl")
        s_pv = sem("s_pv")
        s_oh = sem("s_oh")
        s_ol = sem("s_ol")
        s_store = sem("s_store")

        def col(c):
            return par[:, bass.ds(c, 1)] if not isinstance(c, int) else par[:, c:c + 1]

        def tile(buf, k):
            if isinstance(k, int):
                return buf[:, k, :]
            return buf[:, bass.ds(k, 1), :].rearrange("p a t -> p (a t)")

        def plain(ap):
            return ap.bitcast(F32)

        ident = par[:, C_IDENT:C_IDENT + P]

        def spread(view, dims):
            return bass.AP(tensor=view.tensor, offset=view.offset, ap=[view.ap[0]] + dims)

        bhf = bh[:, :, :].rearrange("p a t -> p (a t)")
        blf = bl[:, :, :].rearrange("p a t -> p (a t)")

        def v_tile(flat, parity):
            at = VT * SEQ + parity * TB * VW
            return flat[:, at:at + TB * VW].rearrange("p (b c) -> p b c", b=TB)

        def v_heads(flat, parity):
            view = v_tile(flat, parity)
            return spread(view, [[VW, TB], [2 * HEAD, 2], [1, HEAD]])

        assert VT * SEQ + 2 * TB * VW <= PT * SEQ and PT * SEQ + SCORES <= FT * SEQ
        pth = bhf[:, PT * SEQ:PT * SEQ + SCORES]
        ptl = blf[:, PT * SEQ:PT * SEQ + SCORES]

        block = ctx.enter_context(nc.Block())

        @block.sync
        def _(sp):
            def load(u, s, dst, src, first=False):
                if not first:
                    sp.wait_ge(s_lo, u - RING + 1)
                sp.dma_start(dst, src).then_inc(s_raw[s], 16)

            def pick(w, i):
                return w[bass.ds(i, 1)].rearrange("a p n -> (a p) n")

            sp.dma_start(par[:], params).then_inc(s_par, 16)
            for n in range(4):
                sp.dma_start(x[:, 2 * n:2 * n + 2, :], xt[:, 2 * n:2 * n + 2, :]).then_inc(s_xin[n], 16)
                if n == 3:
                    for dst, src in ((oh_sb[0:BUCKETS, :], onehot), (cnt_sb[0:2 * PAIRS, :], count),
                                     (rel_sb[0:BUCKETS, :], rel)):
                        sp.dma_start(dst, src).then_inc(s_setup, 16)
                load(n, n, raw[n][:], w_in[n], True)
            sp.dma_start(poolraw, poolw).then_inc(s_pool, 16)
            with sp.Fori(1, GROUPS) as i:
                for s in range(RING):
                    load(U_IN + i * 4 + s, s, raw[s][:], pick(w_in, i * 4 + s))

            def residual_loads(base, w):
                with sp.Fori(0, KT // RING) as i:
                    for s in range(RING):
                        load(base + i * 4 + s, s, raw[s][:], pick(w, i * 4 + s))

            def ffn_loads(layer, up, down):
                with sp.Fori(0, FT // 2) as i:
                    for s in range(RING):
                        load(up + i * 4 + s, s, raw[s][:], pick(w_up, i * 4 + (layer * 2 * FT + s)))
                with sp.Fori(0, KT) as i:
                    at = 0
                    for s, n in enumerate(DOWN_SPLIT):
                        load(down + i * 4 + s, s, raw[s][:, 0:n * P],
                             pick(w_down[:, :, at * P:(at + n) * P], i + layer * KT))
                        at += n

            residual_loads(U_OUT, w_out)
            ffn_loads(0, U_UP0, U_DOWN0)
            with sp.Fori(0, PAIRS) as i:
                for s, (at, n) in enumerate(((0, SLOT), (SLOT, SLOT), (2 * SLOT, SLOT // 2),
                                             (2 * SLOT + SLOT // 2, SLOT // 2))):
                    load(U_QKV + i * 4 + s, s, raw[s][:, 0:n], pick(w_qkv[:, :, at:at + n], i))
            residual_loads(U_WO, w_o)
            ffn_loads(1, U_UP1, U_DOWN1)
            for n in range(KT):
                sp.wait_ge(s_x, 3 * KT + n + 1)
                sp.dma_start(out[n], x[:, n, :]).then_inc(s_store, 16)
            sp.wait_ge(s_store, 16 * KT)

        @block.gpsimd
        def _(pool):
            def rest(u, s):
                pool.wait_ge(s_hi, u + 1)
                nc.gpsimd.tensor_tensor(wl[s][:], raw[s][:], plain(wh[s][:]), ALU.subtract).then_inc(s_lo, 1)

            pool.wait_ge(s_lo, 1)
            for s in range(1, RING):
                rest(s, s)
            with pool.Fori(1, UNITS // RING) as i:
                for s in range(RING):
                    rest(i * RING + s, s)

        @block.scalar
        def _(act):
            def round_unit(q, s, first=False):
                act.wait_ge(s_raw[s], (q + 1) * 16)
                if not first:
                    act.wait_ge(s_unit, q * RING + (s - RING + 1))
                nc.scalar.activation(wh[s][:], raw[s][:], ACT.Copy).then_inc(s_hi, 1)

            def ahead(base, i, j, per=RING):
                round_unit(base // RING + i * (per // RING) + (j + 3) // RING, (j + 3) % RING)

            def prep_first(k):
                act.wait_ge(s_xin[k // 2], 16)
                nc.scalar.activation(xh[:, k, :], x[:, k, :], ACT.Copy, scale=col(C_GAIN + k)).then_inc(s_xh, 1)
                if k >= len(sq_first):
                    act.wait_ge(s_acc, k - len(sq_first) + 2)
                nc.scalar.activation(sq_first[k % len(sq_first)], x[:, k, :], ACT.Square).then_inc(s_sq, 1)

            def prep(norm, k):
                act.wait_ge(s_x, k + ((norm - 1) * KT + 1))
                act.wait_ge(s_acc, k + (norm * (KT + 1) + 1))
                nc.scalar.activation(tile(xh, k), tile(x, k), ACT.Copy,
                                     scale=col(k + (C_GAIN + norm * KT))).then_inc(s_xh, 1)
                nc.scalar.activation(sq[:], tile(x, k), ACT.Square).then_inc(s_sq, 1)

            def keep_rstd(norm):
                act.wait_ge(s_bc, norm + 1)
                nc.scalar.activation(rstd[:], nbank, ACT.Copy).then_inc(s_rstd, 1)

            act.wait_ge(s_par, 16)
            for n in range(3):
                prep_first(2 * n)
                prep_first(2 * n + 1)
                round_unit(0, n, True)
            prep_first(6)
            prep_first(7)
            act.wait_ge(s_pool, 16)
            nc.scalar.activation(bh[:, POOLW, :], poolraw, ACT.Copy).then_inc(s_pwh, 1)

            for g in range(GROUPS):
                if g == 0:
                    round_unit(0, 3, True)
                    keep_rstd(0)
                else:
                    ahead(U_IN, g, 0)
                ahead(U_IN, g, 1)
                act.wait_ge(s_zc, g + 1)
                nc.scalar.activation(cv, zc[:, 2:], ACT.Copy,
                                     scale=col(C_CONVA + TAPS * g + 2)).then_inc(s_cv, 1)
                ahead(U_IN, g, 2)
                act.wait_ge(s_ya, g + 1)
                nc.scalar.activation(bh[:, MIX + g, :], ya, ACT.Copy).then_inc(s_yah, 1)
                ahead(U_IN, g, 3)
                act.wait_ge(s_pd, g + 1)
                nc.scalar.activation(bh[:, POOLED + g, :], pooled, ACT.Copy).then_inc(s_pdh, 1)
                if g == 0:
                    act.wait_ge(s_bv, 1)
                    act.dma_start(bias_rows, bv_sb[0:2 * PAIRS, :]).then_inc(s_rows, 16)
            for g in range(GROUPS):
                act.wait_ge(s_yb, g + 1)
                nc.scalar.activation(bh[:, MIX + GROUPS + g, :], bank[g][:], ACT.Copy,
                                     scale=col(C_PSCALE + g)).then_inc(s_ybh, 1)

            def residual(norm, base):
                for n in range(KT):
                    if n or norm == 1:
                        ahead(base, n // RING, n % RING)
                    if n:
                        prep(norm, n - 1)
                prep(norm, KT - 1)

            def ffn(layer, up, down):
                keep = 2 * layer + 1

                def hidden(i, j, first=False):
                    f = i * 2 + (layer * FT + j)
                    c = C_FFN + layer * FT * 8 + j * 8
                    ahead(up, i, 2 * j)
                    if first:
                        keep_rstd(keep)
                    act.wait_ge(s_z, f * 2 + 1)
                    if not first:
                        act.wait_ge(s_silu, f)
                    nc.scalar.activation(ug, zg[j][:, 2:], ACT.Identity, bias=col(i * 16 + (c + 3)),
                                         scale=col(i * 16 + (c + 2))).then_inc(s_id, 1)
                    ahead(up, i, 2 * j + 1)
                    act.wait_ge(s_z, f * 2 + 2)
                    nc.scalar.activation(uu[j], zu[j][:, 2:], ACT.Identity, bias=col(i * 16 + (c + 7)),
                                         scale=col(i * 16 + (c + 6))).then_inc(s_id, 1)
                    if not first:
                        act.wait_ge(s_h, f)
                        nc.scalar.activation(tile(bh, i * 2 + (j - 1)), hf, ACT.Copy).then_inc(s_hh, 1)
                    act.wait_ge(s_t0, f * 2 + 1)
                    nc.scalar.activation(sg, ug, ACT.Silu).then_inc(s_silu, 1)

                hidden(0, 0, True)
                hidden(0, 1)
                with act.Fori(1, FT // 2) as i:
                    hidden(i, 0)
                    hidden(i, 1)

                ahead(down, 0, 0)
                act.wait_ge(s_h, (layer + 1) * FT)
                nc.scalar.activation(bh[:, FT - 1, :], hf, ACT.Copy).then_inc(s_hh, 1)
                for s in range(1, RING):
                    ahead(down, 0, s)
                with act.Fori(1, KT if layer == 0 else KT - 1) as n:
                    ahead(down, n, 0)
                    if layer == 0:
                        prep(2, n - 1)
                    for s in range(1, RING):
                        ahead(down, n, s)
                if layer == 0:
                    prep(2, KT - 1)
                else:
                    ahead(down, KT - 1, 0)

            residual(1, U_OUT)
            ffn(0, U_UP0, U_DOWN0)

            def stage(p, parity, qkv=True, a=True, b=True):
                if isinstance(p, int) and p == PAIRS:
                    ahead(U_WO, 0, 0)
                if b:
                    round_pt((p - 2) * 2 + 1)
                if qkv:
                    if isinstance(p, int) and p == 0:
                        round_unit(U_QKV // RING, 3)
                        keep_rstd(2)
                    else:
                        ahead(U_QKV, p, 0)
                    squares(p, 0, parity)
                if b:
                    act.wait_ge(s_pv, (p - 2) * 2 + 2)
                    nc.scalar.activation(tile(bh, p - 2 + MIX), obank[:], ACT.Copy).then_inc(s_oh, 1)
                if a:
                    exponentials((p - 1) * 2, 0, p - 1)
                    act.wait_ge(s_vt, p)
                    nc.scalar.activation(v_heads(bhf, 1 - parity),
                                         mbank[:].rearrange("q (b h c) -> q b h c", b=TB, h=2),
                                         ACT.Copy).then_inc(s_vh, 1)
                if qkv:
                    ahead(U_QKV, p, 1)
                if a:
                    round_pt((p - 1) * 2)
                if qkv:
                    squares(p, 1, parity)
                    ahead(U_QKV, p, 2)
                if a:
                    exponentials((p - 1) * 2 + 1, 1, p - 1)
                if qkv:
                    for which, at in ((0, QT), (1, KTILE)):
                        act.wait_ge(s_qn, p * 2 + (which + 1))
                        nc.scalar.activation(bh[:, at + parity, :], (qg, kg)[which],
                                             ACT.Copy).then_inc(s_qh, 1)
                    ahead(U_QKV, p, 3)

            def squares(p, which, parity):
                act.wait_ge(s_unit, p * 4 + (U_QKV + which + 1))
                if not (isinstance(p, int) and p == 0):
                    act.wait_ge(s_st, p)
                nc.scalar.activation((sqq, sqk)[which], bank[which][:], ACT.Square).then_inc(s_qs, 1)
                if not (isinstance(p, int) and p == 0):
                    act.wait_ge(s_ql, p * 2 + (which - 1))
                gain = gqs[:] if which == 0 else col(C_QK + 1)
                nc.scalar.activation((qg, kg)[which], bank[which][:], ACT.Copy,
                                     scale=gain).then_inc(s_qs, 1)

            def exponentials(head, h, pair):
                for n, (b, at, w) in enumerate(PACK):
                    act.wait_ge(s_neg, head * 4 + (n + 1))
                    nc.scalar.activation(sc[:, at:at + w], sc[:, at:at + w], ACT.Exp,
                                         bias=nmax[:, b:b + 1], scale=-1.0,
                                         accum_out=den[:, b:b + 1]).then_inc(s_e, 1)
                if not isinstance(pair, int) or pair < PAIRS - 1:
                    bias_load(h, pair + 1)

            def bias_load(h, pair):
                row = bias_rows[bass.ds(pair * 2 + h, 1), 0:1] if not isinstance(pair, int) else \
                    bias_rows[2 * pair + h:2 * pair + h + 1, 0:1]
                src = bass.AP(tensor=row.tensor, offset=row.offset, ap=[[1, P], [1, SEQ]])
                act.dma_start(toep[h], src).then_inc(s_t[h], 16)

            def round_pt(head):
                act.wait_ge(s_pt, head + 1)
                for at, end in ((0, SEQ), (SEQ, SCORES)):
                    nc.scalar.activation(pth[:, at:end], spt[:, at:end], ACT.Copy).then_inc(s_pth, 1)

            act.wait_ge(s_rows, 16)
            for h in range(2):
                bias_load(h, 0)
            stage(0, 0, a=False, b=False)
            stage(1, 1, b=False)
            with act.Fori(1, PAIRS // 2) as i:
                stage(i * 2, 0)
                stage(i * 2 + 1, 1)
            stage(PAIRS, 0, qkv=False)
            stage(PAIRS + 1, 1, qkv=False, a=False)

            residual(3, U_WO)
            ffn(1, U_UP1, U_DOWN1)

        @block.vector
        def _(dve):
            steps = Steps(dve, s_small)
            link = steps.link

            def rsqrt(width, finish):
                v, half, t = (small[:, n, 0:width] for n in range(3))
                y = small[:, 4, 0:width]
                g = guess[:, 0:width]
                link(nc.vector.tensor_scalar(g, v.bitcast(I32), -0.5, MAGIC, ALU.mult, ALU.add))
                link(nc.vector.tensor_scalar(half, v, -0.5, None, ALU.mult))
                last = g.bitcast(F32)
                for n in range(3):
                    link(nc.vector.tensor_tensor(t, last, last, ALU.mult))
                    link(nc.vector.tensor_tensor(t, t, half, ALU.mult))
                    if n < 2:
                        link(nc.vector.scalar_tensor_tensor(y, t, 1.5, last, ALU.add, ALU.mult))
                    last = y
                finish(t, y)

            def clear_acc():
                nc.vector.memset(acc[:], 0.0).then_inc(s_acc, 1)

            def prep(norm, k, squares=sq[:]):
                dve.wait_ge(s_xh, k + (norm * KT + 1))
                nc.vector.scalar_tensor_tensor(tile(xl, k), tile(x, k), col(k + (C_GAIN + norm * KT)),
                                               plain(tile(xh, k)), ALU.mult, ALU.subtract).then_inc(s_xl, 1)
                dve.wait_ge(s_sq, k + (norm * KT + 1))
                dve.wait_ge(s_acc, k + (norm * (KT + 1) + 1))
                nc.vector.tensor_tensor(acc[:], acc[:], squares, ALU.add).then_inc(s_acc, 1)

            def norm_rsqrt(norm):
                dve.wait_ge(s_ms, norm + 1)
                link(nc.vector.tensor_scalar(small[:, 0, 0:TB], nbank[:, 0:TB], EPS, None, ALU.add))
                if norm == 2:
                    link(nc.vector.tensor_scalar(epsv[:], small[:, 0, 0:TB], EPS, None, ALU.mult))
                rsqrt(TB, lambda t, y: nc.vector.scalar_tensor_tensor(
                    small[:, 3, 0:TB], t, 1.5, y, ALU.add, ALU.mult).then_inc(s_rn, 1))

            dve.wait_ge(s_par, 16)
            link(nc.vector.tensor_scalar(gqs[:], col(C_QK), HEAD ** -0.5, None, ALU.mult))
            clear_acc()
            for k in range(KT):
                prep(0, k, sq_first[k % len(sq_first)])
                if k == 1:
                    dve.wait_ge(s_hi, 1)
                    nc.vector.tensor_tensor(wl[0][:], raw[0][:], plain(wh[0][:]),
                                            ALU.subtract).then_inc(s_lo, 1)
            norm_rsqrt(0)

            dve.wait_ge(s_setup, 48)
            dve.wait_ge(s_bvmm, 2)
            heads = 2 * PAIRS
            link(nc.vector.tensor_tensor(bv_sb[0:heads, 0:SEQ], obank[0:heads, :],
                                         cnt_sb[0:heads, 0:SEQ], ALU.add))
            nc.vector.tensor_tensor(bv_sb[0:heads, SEQ:NVEC], bank[3][0:heads, 0:NVEC - SEQ],
                                    cnt_sb[0:heads, SEQ:NVEC], ALU.add).then_inc(s_bv, 1)

            link(nc.vector.memset(zc[:, 0:2], 0.0))
            for buf in (pin, pa, pb):
                link(nc.vector.memset(buf[:, 0:PAD], 0.0))
            dve.wait_ge(s_pwh, 1)
            nc.vector.tensor_tensor(bl[:, POOLW, :], poolraw, plain(bh[:, POOLW, :]),
                                    ALU.subtract).then_inc(s_pwl, 1)
            dve.wait_ge(s_rstd, 1)
            for g in range(GROUPS):
                def scaled(dst, j):
                    dve.wait_ge(s_unit, U_IN + 4 * g + j + 1)
                    return nc.vector.tensor_tensor(dst, bank[j][:], rstd[:], ALU.mult)

                scaled(hs, 0).then_inc(s_inev, 1)
                scaled(cs, 1).then_inc(s_inev, 1)
                dve.wait_ge(s_inev, 4 * g + 2)
                nc.vector.tensor_tensor(zc[:, 2:], hs, cs, ALU.mult).then_inc(s_zc, 1)
                dve.wait_ge(s_cv, g + 1)
                for tap in (1, 0):
                    link(nc.vector.scalar_tensor_tensor(cv, zc[:, tap:tap + SEQ], col(C_CONVA + TAPS * g + tap),
                                                        cv, ALU.mult, ALU.add))
                scaled(cs, 2).then_inc(s_inev, 1)
                dve.wait_ge(s_inev, 4 * g + 3)
                nc.vector.tensor_tensor(ya, cs, cv, ALU.mult).then_inc(s_ya, 1)
                dve.wait_ge(s_yah, g + 1)
                nc.vector.tensor_tensor(bl[:, MIX + g, :], ya, plain(bh[:, MIX + g, :]),
                                        ALU.subtract).then_inc(s_yal, 1)
                scaled(pin[:, PAD:], 3).then_inc(s_inev, 1)
                dve.wait_ge(s_inev, 4 * g + 4)
                src, n = pin, 1
                for step in range(g + 1):
                    dst = (pa, pb)[step % 2]
                    link(nc.vector.tensor_tensor(dst[:, PAD:], src[:, PAD:], src[:, PAD - n:PAD - n + SEQ], ALU.add))
                    src, n = dst, 2 * n
                assert n == POOL_WINDOWS[g]
                link(nc.vector.scalar_tensor_tensor(pooled, src[:, PAD:], 1.0 / n, pin[:, PAD:],
                                                    ALU.mult, ALU.subtract))
                inv = par[:, C_INV + g * PAD:C_INV + (g + 1) * PAD]
                link(nc.vector.tensor_tensor(small[:, 0, :], src[:, PAD:2 * PAD], inv, ALU.mult))
                nc.vector.tensor_tensor(pooled[:, 0:PAD], small[:, 0, :], pin[:, PAD:2 * PAD],
                                        ALU.subtract).then_inc(s_pd, 1)
                dve.wait_ge(s_pdh, g + 1)
                nc.vector.tensor_tensor(bl[:, POOLED + g, :], pooled, plain(bh[:, POOLED + g, :]),
                                        ALU.subtract).then_inc(s_pdl, 1)
            for g in range(GROUPS):
                dve.wait_ge(s_ybh, g + 1)
                nc.vector.scalar_tensor_tensor(bl[:, MIX + GROUPS + g, :], bank[g][:], col(C_PSCALE + g),
                                               plain(bh[:, MIX + GROUPS + g, :]),
                                               ALU.mult, ALU.subtract).then_inc(s_ybl, 1)

            def add_residual(n, used, block_bank):
                dve.wait_ge(s_unit, used)
                nc.vector.tensor_tensor(tile(x, n), block_bank, tile(x, n), ALU.add).then_inc(s_x, 1)

            def start_norm(norm):
                dve.wait_ge(s_ms, norm)
                clear_acc()

            def residual(phase, base):
                start_norm(phase + 1)
                for n in range(KT):
                    early = phase == 2 and n < RING
                    add_residual(n, base + n + 1, bank[n][:] if early else rbank[n % 2])
                    if n:
                        prep(phase + 1, n - 1)
                prep(phase + 1, KT - 1)
                norm_rsqrt(phase + 1)

            def ffn(layer, up, down):
                for buf in zg + zu:
                    link(nc.vector.memset(buf[:, 0:2], 0.0))
                dve.wait_ge(s_rstd, 2 * layer + 2)

                def hidden(i, j, first=False):
                    f = i * 2 + (layer * FT + j)
                    c = C_FFN + layer * FT * 8 + j * 8
                    for n, buf in enumerate((zg[j], zu[j])):
                        dve.wait_ge(s_unit, i * 4 + (up + 2 * j + n + 1))
                        nc.vector.tensor_tensor(buf[:, 2:], bank[2 * j + n][:], rstd[:],
                                                ALU.mult).then_inc(s_z, 1)
                    if not first:
                        finish(f, 1 - j)
                    for tap, done, before in ((1, s_t1, s_id), (0, s_t0, s_t1)):
                        for n, (z, u) in enumerate(((zg[j], ug), (zu[j], uu[j]))):
                            dve.wait_ge(before, f * 2 + (n + 1))
                            nc.vector.scalar_tensor_tensor(
                                u, z[:, tap:tap + SEQ], col(i * 16 + (c + 4 * n + tap)), u,
                                ALU.mult, ALU.add).then_inc(done, 1)
                    if not first:
                        rest(f, i * 2 + (j - 1))

                def finish(f, j):
                    dve.wait_ge(s_silu, f)
                    dve.wait_ge(s_t0, f * 2)
                    if not isinstance(f, int) or f > 1:
                        dve.wait_ge(s_hl, f - 1)
                    nc.vector.tensor_tensor(hf, sg, uu[j], ALU.mult).then_inc(s_h, 1)

                def rest(f, k):
                    dve.wait_ge(s_hh, f)
                    nc.vector.tensor_tensor(tile(bl, k), hf, plain(tile(bh, k)), ALU.subtract).then_inc(s_hl, 1)

                hidden(0, 0, True)
                hidden(0, 1)
                with dve.Fori(1, FT // 2) as i:
                    hidden(i, 0)
                    hidden(i, 1)
                finish((layer + 1) * FT, 1)
                rest((layer + 1) * FT, FT - 1)

                if layer == 0:
                    start_norm(2)
                    add_residual(0, down + 4, rbank[0])
                    add_residual(1, down + 8, rbank[1])
                    prep(2, 0)
                    with dve.Fori(1, KT // 2) as i:
                        for j in range(2):
                            add_residual(i * 2 + j, i * 8 + (down + 4 * j + 4), rbank[j])
                            prep(2, i * 2 + (j - 1))
                    prep(2, KT - 1)
                    norm_rsqrt(2)
                else:
                    with dve.Fori(0, KT // 2) as i:
                        for j in range(2):
                            add_residual(i * 2 + j, i * 8 + (down + 4 * j + 4), rbank[j])

            residual(0, U_OUT)
            ffn(0, U_UP0, U_DOWN0)

            def scores(head, h, p):
                dve.wait_ge(s_t[h], p * 16)
                dve.wait_ge(s_s, head + 1)
                nc.vector.memset(gate[:], 0.0)
                for b, at, w in PACK:
                    u = w - 1
                    nc.vector.tensor_tensor_reduce(
                        sc[:, at:at + w], spt[:, at:at + w], toep[h][:, u::-1], -1.0, 3e38, ALU.add, ALU.min,
                        nmax[:, b:b + 1]).then_inc(s_neg, 1)

            def probabilities(head):
                dve.wait_ge(s_e, head * 4 + 4)
                link(nc.vector.reciprocal(rden[:], den[:]))
                for b, at, w in PACK:
                    last = nc.vector.tensor_scalar(sc[:, at:at + w], sc[:, at:at + w], rden[:, b:b + 1],
                                                   None, ALU.mult)
                last.then_inc(s_p, 1)

            def rest_pt(head):
                for n, (at, end) in enumerate(((0, SEQ), (SEQ, SCORES))):
                    dve.wait_ge(s_pth, head * 2 + (n + 1))
                    nc.vector.tensor_tensor(ptl[:, at:end], spt[:, at:end], plain(pth[:, at:end]),
                                            ALU.subtract).then_inc(s_ptl, 1)

            def stage(p, parity, qkv=True, a=True, b=True):
                if b:
                    rest_pt((p - 2) * 2 + 1)
                if a:
                    scores((p - 1) * 2, 0, p)
                if b:
                    dve.wait_ge(s_oh, p - 1)
                    k = p - 2 + MIX
                    nc.vector.tensor_tensor(tile(bl, k), obank[:], plain(tile(bh, k)),
                                            ALU.subtract).then_inc(s_ol, 1)
                if a:
                    probabilities((p - 1) * 2)
                    dve.wait_ge(s_vh, p)
                    nc.vector.tensor_tensor(v_heads(blf, 1 - parity),
                                            mbank[:].rearrange("q (b h c) -> q b h c", b=TB, h=2),
                                            plain(v_heads(bhf, 1 - parity)), ALU.subtract).then_inc(s_vl, 1)
                    rest_pt((p - 1) * 2)
                if qkv:
                    dve.wait_ge(s_st, p + 1)
                    ms = small[:, 0, :].rearrange("q (w b h) -> q w b h", w=2, b=TB)
                    link(nc.vector.tensor_tensor(
                        ms, mbank[:, 0:16].rearrange("q (w b h) -> q w b h", w=2, b=TB),
                        spread(epsv[:], [[0, 2], [1, TB], [0, 2]]), ALU.add))
                    rsqrt(16, lambda t, y: widen(0))
                if a:
                    scores((p - 1) * 2 + 1, 1, p)
                if qkv:
                    widen(1)
                    normalise(p, 0, parity)
                if a:
                    probabilities((p - 1) * 2 + 1)
                if qkv:
                    split_qk(p, 0, parity)
                    dve.wait_ge(s_unit, p * 4 + (U_QKV + 4))
                    if a:
                        dve.wait_ge(s_vt, p)
                    nc.vector.tensor_tensor(vf, bank[2][:], rstd[:], ALU.mult).then_inc(s_vf, 1)
                    normalise(p, 1, parity)
                    split_qk(p, 1, parity)

            def widen(which):
                c = which * 2 * TB
                t, y = (spread(small[:, n, c:c + 1], [[1, 2 * TB], [0, HEAD]]) for n in (2, 4))
                wide = (rq, rk)[which].rearrange("q (c e) -> q c e", e=HEAD)
                nc.vector.scalar_tensor_tensor(wide, t, 1.5, y, ALU.add, ALU.mult).then_inc(s_r, 1)

            def normalise(p, which, parity):
                dve.wait_ge(s_rb, p * 2 + (which + 1))
                dve.wait_ge(s_qs, p * 4 + (2 * which + 2))
                buf = (qg, kg)[which]
                nc.vector.tensor_tensor(buf, mbank[:], buf, ALU.mult).then_inc(s_qn, 1)

            def split_qk(p, which, parity):
                at = (QT, KTILE)[which] + parity
                dve.wait_ge(s_qh, p * 2 + (which + 1))
                nc.vector.tensor_tensor(bl[:, at, :], (qg, kg)[which], plain(bh[:, at, :]),
                                        ALU.subtract).then_inc(s_ql, 1)

            for flat in (bhf, blf):
                for parity in range(2):
                    link(nc.vector.memset(plain(v_tile(flat, parity)[:, :, HEAD:2 * HEAD]), 0.0))
            dve.wait_ge(s_rstd, 3)
            stage(0, 0, a=False, b=False)
            stage(1, 1, b=False)
            with dve.Fori(1, PAIRS // 2) as i:
                steps.loop(i, 1, 2 * (1 + 10 + 2))
                stage(i * 2, 0)
                stage(i * 2 + 1, 1)
            steps.end(PAIRS // 2 - 1)
            stage(PAIRS, 0, qkv=False)
            stage(PAIRS + 1, 1, qkv=False, a=False)

            residual(2, U_WO)
            ffn(1, U_UP1, U_DOWN1)

        @block.tensor
        def _(pe):
            mm = nc.tensor.matmul

            def product(dst, s, at, hi, lo, first, last):
                w = slice(at * P, (at + 1) * P)
                mm(dst, wh[s][:, w], hi, start=first, stop=False)
                mm(dst, wh[s][:, w], lo, start=False, stop=False)
                return mm(dst, wl[s][:, w], hi, start=False, stop=last)

            def unit_ready(u):
                pe.wait_ge(s_lo, u + 1)

            def project(dst, u, s, buf_h=xh, buf_l=xl, at=0):
                unit_ready(u)
                for k in range(KT):
                    last = product(dst, s, k, buf_h[:, at + k, :], buf_l[:, at + k, :], k == 0, k == KT - 1)
                last.then_inc(s_unit, 1)

            def norm_stats(norm):
                pe.wait_ge(s_acc, (norm + 1) * (KT + 1))
                for b in range(TB):
                    last = mm(nbank[:, b:b + 1], acc[:, b * P:(b + 1) * P], col(C_ONE), start=True, stop=True)
                last.then_inc(s_ms, 1)

            def norm_spread(norm):
                pe.wait_ge(s_rn, norm + 1)
                for b in range(TB):
                    r = spread(small[:, 3, b:b + 1], [[0, P]])
                    last = nc.tensor.transpose(nbank[:, b * P:(b + 1) * P], r, ident)
                last.then_inc(s_bc, 1)

            def first_two(norm, u):
                for k in range(KT):
                    pe.wait_ge(s_xl, norm * KT + k + 1)
                    if k == 4:
                        norm_stats(norm)
                    if k == KT - 1:
                        norm_spread(norm)
                    for n in range(2):
                        if k == 0:
                            unit_ready(u + n)
                        last = product(bank[n][:], n, k, xh[:, k, :], xl[:, k, :], k == 0, k == KT - 1)
                        if k == KT - 1:
                            last.then_inc(s_unit, 1)

            pe.wait_ge(s_par, 16)
            for k0 in (0, KT // 2):
                for n in range(2):
                    if k0 == 0:
                        unit_ready(U_IN + n)
                    for k in range(k0, k0 + KT // 2):
                        if n == 0:
                            pe.wait_ge(s_xl, k + 1)
                        last = product(bank[n][:], n, k, xh[:, k, :], xl[:, k, :], k == 0, k == KT - 1)
                    if k0:
                        last.then_inc(s_unit, 1)
            norm_stats(0)
            pe.wait_ge(s_setup, 48)
            heads = 2 * PAIRS
            mm(obank[0:heads, :], rel_sb[0:BUCKETS, :], oh_sb[0:BUCKETS, 0:SEQ], start=True, stop=True).then_inc(s_bvmm, 1)
            mm(bank[3][0:heads, 0:NVEC - SEQ], rel_sb[0:BUCKETS, :], oh_sb[0:BUCKETS, SEQ:NVEC],
               start=True, stop=True).then_inc(s_bvmm, 1)
            project(bank[2][:], U_IN + 2, 2)
            norm_spread(0)
            pe.wait_ge(s_bv, 1)
            project(bank[3][:], U_IN + 3, 3)
            with pe.Fori(1, GROUPS) as i:
                for j in range(4):
                    pe.wait_ge(s_inev, i * 4 + (j - 3))
                    project(bank[j][:], i * 4 + (U_IN + j), j)
            unit_ready(U_OUT)
            unit_ready(U_OUT + 1)

            def out_tile(k):
                for n in range(2):
                    last = product(rbank[n], n, k, bh[:, MIX + k, :], bl[:, MIX + k, :], k == 0, k == KT - 1)
                    if k == KT - 1:
                        last.then_inc(s_unit, 1)

            for g in range(GROUPS):
                pe.wait_ge(s_yal, g + 1)
                out_tile(g)
            pe.wait_ge(s_pwl, 1)
            for g in range(GROUPS):
                pe.wait_ge(s_pdl, g + 1)
                pe.wait_ge(s_inev, 4 * GROUPS - 3 + g)
                w = slice(g * P, (g + 1) * P)
                moving = (bh[:, POOLED + g, :], bl[:, POOLED + g, :])
                mm(bank[g][:], bh[:, POOLW, w], moving[0], start=True, stop=False)
                mm(bank[g][:], bh[:, POOLW, w], moving[1], start=False, stop=False)
                mm(bank[g][:], bl[:, POOLW, w], moving[0], start=False, stop=True).then_inc(s_yb, 1)
            for g in range(GROUPS):
                pe.wait_ge(s_ybl, g + 1)
                out_tile(GROUPS + g)

            def residual(phase, base, first=0):
                for n in range(first, KT):
                    if n >= first + 2 or first == 2:
                        pe.wait_ge(s_x, phase * KT + n - 1)
                    project(rbank[n % 2], base + n, n % RING, bh, bl, MIX)

            residual(0, U_OUT, first=2)

            def ffn(layer, up, down):
                norm = 2 * layer + 1
                first_two(norm, up)
                for j in (2, 3):
                    project(bank[j][:], up + j, j)
                with pe.Fori(1, FT // 2) as i:
                    for j in range(4):
                        pe.wait_ge(s_z, i * 4 + (layer * 2 * FT + j - 3))
                        project(bank[j][:], i * 4 + (up + j), j)

                def down_block(i, j, first=False):
                    k = 0
                    for s, count_ in enumerate(DOWN_SPLIT):
                        unit_ready(i * 8 + (down + 4 * j + s))
                        if first:
                            pe.wait_ge(s_hl, layer * FT + k + count_)
                        for at in range(count_):
                            last = product(rbank[j], s, at, bh[:, k, :], bl[:, k, :], k == 0, k == FT - 1)
                            k += 1
                        last.then_inc(s_unit, 1)

                down_block(0, 0, True)
                down_block(0, 1)
                with pe.Fori(1, KT // 2) as i:
                    for j in range(2):
                        pe.wait_ge(s_x, i * 2 + (norm * KT + j - 1))
                        down_block(i, j)

            ffn(0, U_UP0, U_DOWN0)

            def qkv_part(p, which, s, k0, k1, at=0):
                for k in range(k0, k1):
                    last = product(bank[which][:], s, k - at, xh[:, k, :], xl[:, k, :], k == 0, k == KT - 1)
                return last

            def free_bank(p, which):
                if not (isinstance(p, int) and p == 0):
                    if which == 2:
                        pe.wait_ge(s_vf, p)
                    else:
                        pe.wait_ge(s_qs, p * 4 + (2 * which - 2))

            def score_blocks(head, h, parity, first=False):
                pe.wait_ge(s_ql, (head - h) + 2)
                if not first:
                    pe.wait_ge(s_ptl, head * 2)
                rows = slice(h * HEAD, (h + 1) * HEAD)
                for b, at, w in PACK:
                    q = slice(b * P, (b + 1) * P)
                    for n, (qb, kb) in enumerate(((bh, bh), (bh, bl), (bl, bh))):
                        last = mm(spt[:, at:at + w], qb[rows, QT + parity, q], kb[rows, KTILE + parity, 0:w],
                                  start=n == 0, stop=n == 2)
                last.then_inc(s_s, 1)

            def transposes(head):
                pe.wait_ge(s_p, head + 1)
                where = {b: at for b, at, _ in PACK}
                for j in range(TB):
                    dst = where[TB - 1 - j]
                    for b in range(j, TB):
                        last = nc.tensor.transpose(spt[:, dst + (b - j) * P:dst + (b - j + 1) * P],
                                                   sc[:, where[b] + j * P:where[b] + (j + 1) * P], ident)
                last.then_inc(s_pt, 1)

            def outputs(pair, h, parity):
                pe.wait_ge(s_ptl, pair * 4 + (2 * h + 2))
                if h == 0:
                    pe.wait_ge(s_vl, pair + 1)
                    if not (isinstance(pair, int) and pair == 0):
                        pe.wait_ge(s_ol, pair)
                where = {b: (at, w) for b, at, w in PACK}
                for j in range(TB):
                    at, w = where[TB - 1 - j]
                    vc = slice(h * HEAD, h * HEAD + P)
                    vh, vl = v_tile(bhf, parity)[:, j, vc], v_tile(blf, parity)[:, j, vc]
                    for n, (v, pt) in enumerate(((vh, pth), (vh, ptl), (vl, pth))):
                        last = mm(obank[:, j * P:SEQ], v, pt[:, at:at + w],
                                  start=h == 0 and j == 0 and n == 0,
                                  stop=h == 1 and j == TB - 1 and n == 2)
                last.then_inc(s_pv, 1)

            def stage(p, parity, qkv=True, a=True, b=True):
                begin = isinstance(p, int) and p == 0
                if begin:
                    first_two(2, U_QKV)
                elif qkv:
                    free_bank(p, 0)
                    unit_ready(p * 4 + U_QKV)
                    qkv_part(p, 0, 0, 0, KT // 2)
                if b:
                    transposes((p - 2) * 2 + 1)
                if qkv and not begin:
                    qkv_part(p, 0, 0, KT // 2, KT).then_inc(s_unit, 1)
                if b:
                    outputs(p - 2, 1, parity)
                if a:
                    score_blocks((p - 1) * 2, 0, 1 - parity, first=not b)
                    turn_v(p - 1)
                if qkv and not begin:
                    free_bank(p, 1)
                    unit_ready(p * 4 + (U_QKV + 1))
                    qkv_part(p, 1, 1, 0, KT).then_inc(s_unit, 1)
                if a:
                    transposes((p - 1) * 2)
                if qkv:
                    free_bank(p, 2)
                    unit_ready(p * 4 + (U_QKV + 2))
                    qkv_part(p, 2, 2, 0, KT // 2).then_inc(s_unit, 1)
                    pe.wait_ge(s_qs, p * 4 + 3)
                    if a:
                        pe.wait_ge(s_vl, p)
                    for which, src in enumerate((sqq, sqk)):
                        for n in range(TB):
                            c = which * 2 * TB + 2 * n
                            last = mm(mbank[:, c:c + 2], src[:, n * P:(n + 1) * P],
                                      par[:, C_HEAD:C_HEAD + 2], start=True, stop=True)
                    last.then_inc(s_st, 1)
                if a:
                    outputs(p - 1, 0, 1 - parity)
                    score_blocks((p - 1) * 2 + 1, 1, 1 - parity)
                if qkv:
                    if not begin:
                        spread_norm(p, 0)
                    unit_ready(p * 4 + (U_QKV + 3))
                    qkv_part(p, 2, 3, KT // 2, KT, at=KT // 2).then_inc(s_unit, 1)
                    if begin:
                        spread_norm(p, 0)
                    spread_norm(p, 1)

            def turn_v(pair):
                pe.wait_ge(s_vf, pair + 1)
                pe.wait_ge(s_qn, pair * 2 + 2)
                for n in range(TB):
                    last = nc.tensor.transpose(mbank[:, n * P:(n + 1) * P], vf[:, n * P:(n + 1) * P], ident)
                last.then_inc(s_vt, 1)

            def spread_norm(p, which):
                pe.wait_ge(s_r, p * 2 + (which + 1))
                if which:
                    pe.wait_ge(s_qn, p * 2 + 1)
                for n in range(TB):
                    last = nc.tensor.transpose(mbank[:, n * P:(n + 1) * P],
                                               (rq, rk)[which][:, n * P:(n + 1) * P], ident)
                last.then_inc(s_rb, 1)

            stage(0, 0, a=False, b=False)
            stage(1, 1, b=False)
            with pe.Fori(1, PAIRS // 2) as i:
                stage(i * 2, 0)
                stage(i * 2 + 1, 1)
            def wo_part(n, k0, k1):
                if k0 == 0:
                    unit_ready(U_WO + n)
                for k in range(k0, k1):
                    pe.wait_ge(s_ol, k + 1)
                    last = product(bank[n][:], n, k, bh[:, MIX + k, :], bl[:, MIX + k, :], k == 0, k == KT - 1)
                if k1 == KT:
                    last.then_inc(s_unit, 1)

            end = PAIRS - 1
            pe.wait_ge(s_qs, 4 * PAIRS)
            wo_part(0, 0, 3)
            transposes(2 * end - 1)
            wo_part(0, 3, 5)
            outputs(end - 1, 1, 0)
            score_blocks(2 * end, 0, 1)
            turn_v(end)
            wo_part(0, 5, 6)
            wo_part(1, 0, 5)
            transposes(2 * end)
            wo_part(1, 5, 7)
            wo_part(0, 6, 7)
            outputs(end, 0, 1)
            score_blocks(2 * end + 1, 1, 1)
            wo_part(2, 0, 7)
            transposes(2 * end + 1)
            wo_part(3, 0, 4)
            outputs(end, 1, 1)
            for n in range(3):
                wo_part(n, 7, 8)
            wo_part(3, 4, 8)
            residual(2, U_WO, first=4)
            ffn(1, U_UP1, U_DOWN1)


def column_tiles(w):
    k, n = w.shape
    return w.reshape(k // P, P, n // P, P).transpose(2, 1, 0, 3).reshape(n // P, P, k)


def pack_params(even_norm, odd_norm, ffn_norm, q_norm, k_norm, conv_a, pool_scale, ffn_w, ffn_b):
    out = np.zeros((P, NPAR), np.float32)
    for n, g in enumerate((even_norm[0], ffn_norm[0], odd_norm[0], ffn_norm[1])):
        out[:, C_GAIN + n * KT:C_GAIN + (n + 1) * KT] = g.reshape(KT, P).T
    out[:, C_QK] = np.concatenate([q_norm[0]] * 2)
    out[:, C_QK + 1] = np.concatenate([k_norm[0]] * 2)
    out[:, C_CONVA:C_PSCALE] = conv_a[0].reshape(TAPS, GROUPS, P).transpose(2, 1, 0).reshape(P, -1)
    out[:, C_PSCALE:C_FFN] = pool_scale[0].reshape(GROUPS, P).T
    taps = np.concatenate([ffn_w, ffn_b[:, None]], axis=1)
    taps = taps.reshape(2, TAPS + 1, 2, FT, P).transpose(4, 0, 3, 2, 1)
    out[:, C_FFN:C_ONE] = taps.reshape(P, -1)
    out[:, C_ONE] = 1.0 / D
    out[:HEAD, C_HEAD] = 1.0 / HEAD
    out[HEAD:, C_HEAD + 1] = 1.0 / HEAD
    for g, n in enumerate(POOL_WINDOWS):
        out[:, C_INV + g * PAD:C_INV + (g + 1) * PAD] = 1.0 / np.minimum(np.arange(1, PAD + 1), n)
    out[:, C_IDENT:] = np.eye(P, dtype=np.float32)
    return out


def build(nc, shapes):
    ins = [nc.dram_tensor(name, shape, F32, kind="ExternalInput").ap() for name, shape in shapes.items()]
    out = nc.dram_tensor("out_t", [KT, P, SEQ], F32, kind="ExternalOutput").ap()
    trunk(nc, *ins, out)


def kernel(x, rel_bias, even_norm, even_w_in, even_conv_w, even_pool_w, even_pool_scale, even_w_out,
           odd_norm, odd_w_qkv, odd_q_norm, odd_k_norm, odd_w_o, ffn_norm, ffn_w_up, ffn_conv_w,
           ffn_conv_b, ffn_w_down):
    import concourse.bacc as bacc
    from concourse.bass_utils import run_bass_kernel_spmd

    onehot, count = shape_constants()
    a = np.asarray
    tiles_in = column_tiles(a(even_w_in)[0]).reshape(4, GROUPS, P, D)
    up = np.stack([column_tiles(w) for w in a(ffn_w_up)])
    qkv = column_tiles(a(odd_w_qkv)[0]).reshape(3, PAIRS, P, D)
    arrays = {
        "xt": a(x)[0].T.reshape(KT, P, SEQ).transpose(1, 0, 2),
        "params": pack_params(a(even_norm), a(odd_norm), a(ffn_norm), a(odd_q_norm), a(odd_k_norm),
                              a(even_conv_w), a(even_pool_scale), a(ffn_conv_w), a(ffn_conv_b)),
        "onehot": onehot,
        "count": count,
        "rel": a(rel_bias),
        "poolw": a(even_pool_w)[0].transpose(1, 0, 2).reshape(P, GROUPS * P),
        "w_in": tiles_in[[0, 2, 1, 3]].transpose(1, 0, 2, 3).reshape(4 * GROUPS, P, D),
        "w_out": column_tiles(a(even_w_out)[0]),
        "w_up": up.reshape(2, 2, FT, P, D).transpose(0, 2, 1, 3, 4).reshape(4 * FT, P, D),
        "w_down": np.concatenate([column_tiles(w) for w in a(ffn_w_down)]),
        "w_qkv": qkv.transpose(1, 2, 0, 3).reshape(PAIRS, P, 3 * D),
        "w_o": column_tiles(a(odd_w_o)[0]),
    }
    arrays = {name: np.ascontiguousarray(v) for name, v in arrays.items()}
    nc = bacc.Bacc("TRN2", target_bir_lowering=False, num_devices=1, dynamic_dma_scratch_size=1024)
    build(nc, {name: list(v.shape) for name, v in arrays.items()})
    result = run_bass_kernel_spmd(nc, [arrays], core_ids=[0])
    got = result.results[0]["out_t"]
    return np.ascontiguousarray(got.reshape(D, SEQ).T)[None]
```

```python
from contextlib import ExitStack
import math

import numpy as np

import concourse.bass as bass
from concourse import mybir

F32 = mybir.dt.float32
F32R = mybir.dt.float32r
I32 = mybir.dt.int32
ALU = mybir.AluOpType
ACT = mybir.ActivationFunctionType

P = 128
SEQ = 512
D = 1024
KT = D // P
TB = SEQ // P
D_FF = 2816
FT = D_FF // P
A_WIDTH = D // 2
GROUPS = A_WIDTH // P
POOL_WINDOWS = (2, 4, 8, 16)
PAD = max(POOL_WINDOWS)
TAPS = 3
HEAD = 64
PAIRS = D // (2 * HEAD)
DILATED = ((128, 1), (512, 4), (2048, 16))
BUCKETS = 32
REL_MAX = 2048
EPS = 1e-6
MASKED = -1e30
NVEC = SEQ + 2 * P

RING = 4
SLOT = KT * P
DOWN_SPLIT = (6, 6, 5, 5)
assert sum(DOWN_SPLIT) == FT

U_IN = 0
U_OUT = U_IN + 4 * GROUPS
U_UP0 = U_OUT + KT
U_DOWN0 = U_UP0 + 2 * FT
U_QKV = U_DOWN0 + 4 * KT
U_WO = U_QKV + 4 * PAIRS
U_UP1 = U_WO + KT
U_DOWN1 = U_UP1 + 2 * FT
UNITS = U_DOWN1 + 4 * KT
assert all(u % RING == 0 for u in (U_OUT, U_UP0, U_DOWN0, U_QKV, U_WO, U_UP1, U_DOWN1, UNITS))

C_GAIN = 0
C_QK = C_GAIN + 4 * KT
C_CONVA = C_QK + 2
C_PSCALE = C_CONVA + TAPS * GROUPS
C_FFN = C_PSCALE + GROUPS
C_ONE = C_FFN + 2 * FT * 8
C_HEAD = C_ONE + 1
C_INV = C_HEAD + 2
C_IDENT = C_INV + GROUPS * PAD
NPAR = C_IDENT + P

MIX = 0
POOLED = 8
POOLW = 12
QT = 8
KTILE = 12
KREST = 8
VT = 10
PT = 16
VW = 4 * HEAD

SCORES = sum(P * (b + 1) for b in range(TB))
PACK = [(3, 0, 512), (2, 512, 384), (0, 896, 128), (1, 1024, 256)]
MAGIC = float(0x5F3759DF)
WARM = 3


def relative_bucket(dist):
    exact = BUCKETS // 2
    if dist < exact:
        return dist
    large = exact + int(math.log(dist / exact) / math.log(REL_MAX / exact) * (BUCKETS - exact))
    return min(large, BUCKETS - 1)


def shape_constants():
    onehot = np.zeros((BUCKETS, NVEC), np.float32)
    count = np.full((2 * PAIRS, NVEC), MASKED, np.float32)
    for y in range(P - 1, P - 1 + SEQ):
        dist = y - (P - 1)
        n = sum(dist % dil == 0 and dist <= window for window, dil in DILATED)
        if n:
            onehot[relative_bucket(dist), y] = 1.0
            count[:, y] = math.log(n)
    return onehot, count


class Steps:

    def __init__(self, eng, sem):
        self.eng, self.sem, self.base, self.n = eng, sem, 0, 0

    def link(self, instruction):
        self.n += 1
        instruction.then_inc(self.sem, 1)
        self.eng.wait_ge(self.sem, self.base + self.n)

    def loop(self, i, first, per):
        self.before = self.base + self.n
        self.base, self.n, self.per = self.before + (i - first) * per, 0, per

    def end(self, rounds):
        assert self.n == self.per, (self.n, self.per)
        self.base, self.n = self.before + rounds * self.per, 0


def trunk(nc, xt, params, onehot, count, rel, poolw, w_in, w_out, w_up, w_down, w_qkv, w_o, out):
    bias_rows = nc.dram_tensor("bias_rows", [2 * PAIRS, NVEC], F32, kind="Internal").ap()
    with ExitStack() as ctx:
        def sb(name, shape, dt=F32):
            return ctx.enter_context(nc.sbuf_tensor(name, shape, dt))

        def sem(name):
            return ctx.enter_context(nc.semaphore(name))

        x = sb("x", [P, KT, SEQ])
        xh = sb("xh", [P, KT, SEQ], F32R)
        xl = sb("xl", [P, KT, SEQ], F32R)
        bh = sb("bh", [P, FT, SEQ], F32R)
        bl = sb("bl", [P, FT, SEQ], F32R)
        raw = [sb(f"raw{s}", [P, SLOT]) for s in range(RING)]
        wh = [sb(f"wh{s}", [P, SLOT], F32R) for s in range(RING)]
        wl = [sb(f"wl{s}", [P, SLOT], F32R) for s in range(RING)]
        kept_h = sb("kept_h", [P, P], F32R)
        kept_l = sb("kept_l", [P, P], F32R)
        par = sb("par", [P, NPAR])
        rstd = sb("rstd", [P, SEQ])
        acc = sb("acc", [P, SEQ])
        sq = sb("sq", [P, SEQ])
        small = sb("small", [P, 5, 16])
        guess = sb("guess", [P, 16], I32)
        epsv = sb("epsv", [P, TB])
        gqs = sb("gqs", [P, 1])
        work = sb("work", [P, 6200])

        def tiles(sizes):
            at, views = 0, []
            for n in sizes:
                views.append(work[:, at:at + n])
                at += n
            assert at <= 6200
            return views

        hs, zc, cv, ya, pin, pa, pb, pooled, cs, poolraw = tiles(
            [SEQ, SEQ + 2, SEQ, SEQ, SEQ + PAD, SEQ + PAD, SEQ + PAD, SEQ, SEQ, GROUPS * P])
        zg0, zu0, zg1, zu1, ug, uu0, uu1, sg, hf = tiles([SEQ + 2] * 4 + [SEQ] * 5)
        zg, zu, uu = [zg0, zg1], [zu0, zu1], [uu0, uu1]
        sc, t0, t1, vf, sqq, sqk, qg, kg, rq, rk = tiles([SCORES] + [SEQ] * 9)
        toep = [t0, t1]
        left_over = sq[:]
        oh_sb, cnt_sb, rel_sb = tiles([NVEC, NVEC, 2 * PAIRS])
        bv_sb = sb("bv_sb", [P, NVEC])
        sq_first = [sq[:], pooled, cs, pin[:, 0:SEQ]]
        nmax = sb("nmax", [P, TB])
        gate = sb("gate", [P, 1])
        spare = sb("spare", [P, 1])
        den = sb("den", [P, TB])
        rden = sb("rden", [P, TB])

        bank = [ctx.enter_context(nc.psum_tensor(f"bank{b}", [P, SEQ], F32)) for b in range(4)]
        spt = ctx.enter_context(nc.psum_tensor("spt", [P, 3 * SEQ], F32))
        obank = ctx.enter_context(nc.psum_tensor("obank", [P, SEQ], F32))
        rbank = [spt[:, 0:SEQ], spt[:, SEQ:2 * SEQ]]
        nbank = spt[:, 2 * SEQ:3 * SEQ]
        mbank = bank[3]

        s_par = sem("s_par")
        s_par_b = sem("s_par_b")
        s_warm = sem("s_warm")
        s_xin = [sem(f"s_xin{n}") for n in range(4)]
        s_pool = sem("s_pool")
        s_setup = sem("s_setup")
        s_bvmm = sem("s_bvmm")
        s_bv = sem("s_bv")
        s_rows = sem("s_rows")
        s_raw = [sem(f"s_raw{s}") for s in range(RING)]
        s_raw_a = sem("s_raw_a")
        s_hi_a = sem("s_hi_a")
        s_lo_a = sem("s_lo_a")
        s_hi = sem("s_hi")
        s_lo = sem("s_lo")
        s_unit = sem("s_unit")
        s_x = sem("s_x")
        s_xh = sem("s_xh")
        s_xl = sem("s_xl")
        s_sq = sem("s_sq")
        s_acc = sem("s_acc")
        s_ms = sem("s_ms")
        s_rn = sem("s_rn")
        s_bc = sem("s_bc")
        s_rstd = sem("s_rstd")
        s_small = sem("s_small")
        s_inev = sem("s_inev")
        s_zc = sem("s_zc")
        s_cv = sem("s_cv")
        s_ya = sem("s_ya")
        s_yah = sem("s_yah")
        s_yal = sem("s_yal")
        s_pd = sem("s_pd")
        s_pdh = sem("s_pdh")
        s_pdl = sem("s_pdl")
        s_pwh = sem("s_pwh")
        s_pwl = sem("s_pwl")
        s_yb = sem("s_yb")
        s_ybh = sem("s_ybh")
        s_ybl = sem("s_ybl")
        s_z = sem("s_z")
        s_id = sem("s_id")
        s_t1 = sem("s_t1")
        s_t0 = sem("s_t0")
        s_silu = sem("s_silu")
        s_h = sem("s_h")
        s_hh = sem("s_hh")
        s_hl = sem("s_hl")
        s_t = [sem("s_ta"), sem("s_tb")]
        s_vf = sem("s_vf")
        s_vt = sem("s_vt")
        s_vh = sem("s_vh")
        s_vl = sem("s_vl")
        s_qs = sem("s_qs")
        s_st = sem("s_st")
        s_r = sem("s_r")
        s_rb = sem("s_rb")
        s_qn = sem("s_qn")
        s_qh = sem("s_qh")
        s_kh = sem("s_kh")
        s_ql = sem("s_ql")
        s_s = sem("s_s")
        s_neg = sem("s_neg")
        s_e = sem("s_e")
        s_p = sem("s_p")
        s_pt = sem("s_pt")
        s_pth = sem("s_pth")
        s_ptl = sem("s_ptl")
        s_pv = sem("s_pv")
        s_oh = sem("s_oh")
        s_of = sem("s_of")
        s_ol = sem("s_ol")
        s_kept = sem("s_kept")
        s_wo0 = sem("s_wo0")
        s_store = sem("s_store")

        def col(c):
            return par[:, bass.ds(c, 1)] if not isinstance(c, int) else par[:, c:c + 1]

        def tile(buf, k):
            if isinstance(k, int):
                return buf[:, k, :]
            return buf[:, bass.ds(k, 1), :].rearrange("p a t -> p (a t)")

        def plain(ap):
            return ap.bitcast(F32)

        ident = par[:, C_IDENT:C_IDENT + P]

        def half(h):
            return slice(h * HEAD, (h + 1) * HEAD)

        def spread(view, dims):
            return bass.AP(tensor=view.tensor, offset=view.offset, ap=[view.ap[0]] + dims)

        bhf = bh[:, :, :].rearrange("p a t -> p (a t)")
        blf = bl[:, :, :].rearrange("p a t -> p (a t)")

        def v_tile(parity):
            at = VT * SEQ + parity * TB * VW
            return blf[:, at:at + TB * VW]

        def v_heads(parity, lo):
            start, step = (HEAD, HEAD) if lo else (0, 3 * HEAD)
            return spread(v_tile(parity)[:, start:start + 1], [[VW, TB], [step, 2], [1, HEAD]])

        assert VT * SEQ + 2 * TB * VW <= PT * SEQ and PT * SEQ + SCORES <= FT * SEQ
        assert QT + 4 <= KTILE and KTILE + 4 <= PT and KREST + 2 <= VT
        pth = bhf[:, PT * SEQ:PT * SEQ + SCORES]
        ptl = blf[:, PT * SEQ:PT * SEQ + SCORES]

        block = ctx.enter_context(nc.Block())

        @block.sync
        def _(sp):
            def load(u, s, dst, src, first=False):
                if not first:
                    sp.wait_ge(s_lo, u - RING + 1)
                sp.dma_start(dst, src).then_inc(s_raw[s], 16)

            def pick(w, i):
                return w[bass.ds(i, 1)].rearrange("a p n -> (a p) n")

            def x_load(n):
                sp.dma_start(x[:, 2 * n:2 * n + 2, :], xt[:, 2 * n:2 * n + 2, :]).then_inc(s_xin[n], 16)

            sp.dma_start(par[:, 0:C_FFN], params[:, 0:C_FFN]).then_inc(s_par, 16)
            x_load(0)
            sp.dma_start(raw[0][:, 0:SLOT // 2], w_in[0, :, 0:SLOT // 2]).then_inc(s_raw_a, 16)
            load(0, 0, raw[0][:, SLOT // 2:], w_in[0, :, SLOT // 2:], True)
            x_load(1)
            load(1, 1, raw[1][:], w_in[1], True)
            x_load(2)
            x_load(3)
            load(2, 2, raw[2][:], w_in[2], True)
            sp.dma_start(par[:, C_FFN:], params[:, C_FFN:]).then_inc(s_par_b, 16)
            load(3, 3, raw[3][:], w_in[3], True)
            for dst, src in ((oh_sb[0:BUCKETS, :], onehot), (cnt_sb[0:2 * PAIRS, :], count),
                             (rel_sb[0:BUCKETS, :], rel)):
                sp.dma_start(dst, src).then_inc(s_setup, 16)
            sp.dma_start(poolraw, poolw).then_inc(s_pool, 16)
            sp.wait_ge(s_lo_a, 2)
            with sp.Fori(1, GROUPS) as i:
                for s in range(RING):
                    load(U_IN + i * 4 + s, s, raw[s][:], pick(w_in, i * 4 + s))

            def residual_loads(base, w):
                with sp.Fori(0, KT // RING) as i:
                    for s in range(RING):
                        load(base + i * 4 + s, s, raw[s][:], pick(w, i * 4 + s))

            def ffn_loads(layer, up, down):
                with sp.Fori(0, FT // 2) as i:
                    for s in range(RING):
                        load(up + i * 4 + s, s, raw[s][:], pick(w_up, i * 4 + (layer * 2 * FT + s)))
                with sp.Fori(0, KT) as i:
                    at = 0
                    for s, n in enumerate(DOWN_SPLIT):
                        load(down + i * 4 + s, s, raw[s][:, 0:n * P],
                             pick(w_down[:, :, at * P:(at + n) * P], i + layer * KT))
                        at += n

            residual_loads(U_OUT, w_out)
            ffn_loads(0, U_UP0, U_DOWN0)
            with sp.Fori(0, PAIRS) as i:
                for s, (at, n) in enumerate(((0, SLOT), (SLOT, SLOT), (2 * SLOT, SLOT // 2),
                                             (2 * SLOT + SLOT // 2, SLOT // 2))):
                    load(U_QKV + i * 4 + s, s, raw[s][:, 0:n], pick(w_qkv[:, :, at:at + n], i))
            residual_loads(U_WO, w_o)
            ffn_loads(1, U_UP1, U_DOWN1)
            for n in range(KT):
                sp.wait_ge(s_x, 3 * KT + n + 1)
                sp.dma_start(out[n], x[:, n, :]).then_inc(s_store, 16)
            sp.wait_ge(s_store, 16 * KT)

        @block.gpsimd
        def _(pool):
            def rest(u, s):
                pool.wait_ge(s_hi, u + 1)
                nc.gpsimd.tensor_tensor(wl[s][:], raw[s][:], plain(wh[s][:]), ALU.subtract).then_inc(s_lo, 1)

            for s in range(2):
                pool.wait_ge(s_hi, s + 1)
                second = slice(SLOT // 2, SLOT)
                nc.gpsimd.tensor_tensor(wl[s][:, second], raw[s][:, second], plain(wh[s][:, second]),
                                        ALU.subtract).then_inc(s_lo, 1)
            for s in range(2, RING):
                rest(s, s)
            with pool.Fori(1, UNITS // RING) as i:
                for s in range(RING):
                    rest(i * RING + s, s)

        @block.scalar
        def _(act):
            def round_unit(q, s, first=False):
                act.wait_ge(s_raw[s], (q + 1) * 16)
                if not first:
                    act.wait_ge(s_unit, q * RING + (s - RING + 1))
                nc.scalar.activation(wh[s][:], raw[s][:], ACT.Copy).then_inc(s_hi, 1)

            def ahead(base, i, j, per=RING):
                round_unit(base // RING + i * (per // RING) + (j + 3) // RING, (j + 3) % RING)

            def round_first(k):
                act.wait_ge(s_xin[k // 2], 16)
                nc.scalar.activation(xh[:, k, :], x[:, k, :], ACT.Copy, scale=col(C_GAIN + k)).then_inc(s_xh, 1)

            def square_first(k):
                if k >= len(sq_first):
                    act.wait_ge(s_acc, k - len(sq_first) + 2)
                nc.scalar.activation(sq_first[k % len(sq_first)], x[:, k, :], ACT.Square).then_inc(s_sq, 1)

            def prep(norm, k):
                act.wait_ge(s_x, k + ((norm - 1) * KT + 1))
                act.wait_ge(s_acc, k + (norm * (KT + 1) + 1))
                nc.scalar.activation(tile(xh, k), tile(x, k), ACT.Copy,
                                     scale=col(k + (C_GAIN + norm * KT))).then_inc(s_xh, 1)
                nc.scalar.activation(sq[:], tile(x, k), ACT.Square).then_inc(s_sq, 1)

            def keep_rstd(norm):
                act.wait_ge(s_bc, norm + 1)
                nc.scalar.activation(rstd[:], nbank, ACT.Copy).then_inc(s_rstd, 1)

            act.wait_ge(s_small, 1)
            nc.scalar.activation(spare[:], gate[:], ACT.Copy)
            act.wait_ge(s_par, 16)
            round_first(0)
            act.wait_ge(s_raw_a, 16)
            nc.scalar.activation(wh[0][:, 0:SLOT // 2], raw[0][:, 0:SLOT // 2], ACT.Copy).then_inc(s_hi_a, 1)
            round_first(1)
            act.wait_ge(s_raw[0], 16)
            nc.scalar.activation(wh[0][:, SLOT // 2:], raw[0][:, SLOT // 2:], ACT.Copy).then_inc(s_hi, 1)
            round_first(2)
            round_first(3)
            round_unit(0, 1, True)
            for k in range(4, KT):
                round_first(k)
            round_unit(0, 2, True)
            for k in range(KT):
                square_first(k)
                if k == 3:
                    round_unit(0, 3, True)
            act.wait_ge(s_par_b, 16)
            act.wait_ge(s_pool, 16)
            nc.scalar.activation(bh[:, POOLW, :], poolraw, ACT.Copy).then_inc(s_pwh, 1)

            for g in range(GROUPS):
                if g == 0:
                    keep_rstd(0)
                else:
                    ahead(U_IN, g, 0)
                ahead(U_IN, g, 1)
                act.wait_ge(s_zc, g + 1)
                nc.scalar.activation(cv, zc[:, 2:], ACT.Copy,
                                     scale=col(C_CONVA + TAPS * g + 2)).then_inc(s_cv, 1)
                ahead(U_IN, g, 2)
                act.wait_ge(s_ya, g + 1)
                nc.scalar.activation(bh[:, MIX + g, :], ya, ACT.Copy).then_inc(s_yah, 1)
                ahead(U_IN, g, 3)
                act.wait_ge(s_pd, g + 1)
                nc.scalar.activation(bh[:, POOLED + g, :], pooled, ACT.Copy).then_inc(s_pdh, 1)
                if g == 0:
                    act.wait_ge(s_bv, 1)
                    act.dma_start(bias_rows, bv_sb[0:2 * PAIRS, :]).then_inc(s_rows, 16)
            for g in range(GROUPS):
                act.wait_ge(s_yb, g + 1)
                nc.scalar.activation(bh[:, MIX + GROUPS + g, :], bank[g][:], ACT.Copy,
                                     scale=col(C_PSCALE + g)).then_inc(s_ybh, 1)

            def residual(norm, base):
                steps = range(KT) if norm == 1 else (None, 2, 3, 4, None, 5, 6, 7)
                for n, m in enumerate(steps):
                    if m is not None:
                        ahead(base, m // RING, m % RING)
                    if n:
                        prep(norm, n - 1)
                prep(norm, KT - 1)

            def ffn(layer, up, down):
                keep = 2 * layer + 1

                def hidden(i, j, first=False):
                    f = i * 2 + (layer * FT + j)
                    c = C_FFN + layer * FT * 8 + j * 8
                    ahead(up, i, 2 * j)
                    if first:
                        keep_rstd(keep)
                    act.wait_ge(s_z, f * 2 + 1)
                    if not first:
                        act.wait_ge(s_silu, f)
                    nc.scalar.activation(ug, zg[j][:, 2:], ACT.Identity, bias=col(i * 16 + (c + 3)),
                                         scale=col(i * 16 + (c + 2))).then_inc(s_id, 1)
                    ahead(up, i, 2 * j + 1)
                    act.wait_ge(s_z, f * 2 + 2)
                    nc.scalar.activation(uu[j], zu[j][:, 2:], ACT.Identity, bias=col(i * 16 + (c + 7)),
                                         scale=col(i * 16 + (c + 6))).then_inc(s_id, 1)
                    if not first:
                        act.wait_ge(s_h, f)
                        nc.scalar.activation(tile(bh, i * 2 + (j - 1)), hf, ACT.Copy).then_inc(s_hh, 1)
                    act.wait_ge(s_t0, f * 2 + 1)
                    nc.scalar.activation(sg, ug, ACT.Silu).then_inc(s_silu, 1)

                hidden(0, 0, True)
                hidden(0, 1)
                with act.Fori(1, FT // 2) as i:
                    hidden(i, 0)
                    hidden(i, 1)

                ahead(down, 0, 0)
                act.wait_ge(s_h, (layer + 1) * FT)
                nc.scalar.activation(bh[:, FT - 1, :], hf, ACT.Copy).then_inc(s_hh, 1)
                for s in range(1, RING):
                    ahead(down, 0, s)
                with act.Fori(1, KT if layer == 0 else KT - 1) as n:
                    ahead(down, n, 0)
                    if layer == 0:
                        prep(2, n - 1)
                    for s in range(1, RING):
                        ahead(down, n, s)
                if layer == 0:
                    prep(2, KT - 1)
                else:
                    ahead(down, KT - 1, 0)

            residual(1, U_OUT)
            ffn(0, U_UP0, U_DOWN0)

            def stage(p, parity, qkv=True, a=True, b=True):
                if b:
                    round_pt((p - 2) * 2 + 1)
                    if not isinstance(p, int) or p <= PAIRS:
                        round_output(p - 2, 0)
                if a:
                    ahead(U_QKV, p - 1, 3)
                if isinstance(p, int) and p == PAIRS:
                    ahead(U_WO, 0, 0)
                if qkv:
                    if isinstance(p, int) and p == 0:
                        round_unit(U_QKV // RING, 3)
                        keep_rstd(2)
                    else:
                        ahead(U_QKV, p, 0)
                    squares(p, 0, parity)
                if b:
                    round_output(p - 2, 1)
                if a:
                    exponentials((p - 1) * 2, 0, p - 1)
                    act.wait_ge(s_vt, p)
                    nc.scalar.activation(v_heads(1 - parity, lo=False),
                                         mbank[:].rearrange("q (b h c) -> q b h c", b=TB, h=2),
                                         ACT.Copy).then_inc(s_vh, 1)
                if qkv:
                    ahead(U_QKV, p, 1)
                    squares(p, 1, parity)
                if a:
                    round_pt((p - 1) * 2)
                if isinstance(p, int) and p == PAIRS:
                    keep_w_o()
                if qkv:
                    ahead(U_QKV, p, 2)
                    act.wait_ge(s_qn, p * 2 + 1)
                    for h in range(2):
                        rows = half(h)
                        nc.scalar.activation(bh[rows, QT + 2 * parity + h, :], qg[rows, :],
                                             ACT.Copy).then_inc(s_qh, 1)
                if a:
                    exponentials((p - 1) * 2 + 1, 1, p - 1)
                if isinstance(p, int) and p == PAIRS:
                    round_output(p - 1, 0)
                    ahead(U_WO, 0, 1)
                if qkv:
                    act.wait_ge(s_qn, p * 2 + 2)
                    for h in range(2):
                        for copy in (h, 1 - h):
                            nc.scalar.activation(bh[half(copy), KTILE + 2 * parity + h, :],
                                                 kg[half(h), :], ACT.Copy).then_inc(s_kh, 1)

            def keep_w_o():
                act.wait_ge(s_lo, U_WO + 1)
                at = slice((KT - 1) * P, KT * P)
                nc.scalar.activation(kept_h[:], plain(wh[0][:, at]), ACT.Copy).then_inc(s_kept, 1)
                nc.scalar.activation(kept_l[:], plain(wl[0][:, at]), ACT.Copy).then_inc(s_kept, 1)

            def round_output(pair, h):
                rows = half(h)
                act.wait_ge(s_pv, pair * 2 + (h + 1))
                nc.scalar.activation(tile(bh, pair + MIX)[rows, :], obank[rows, :],
                                     ACT.Copy).then_inc(s_oh, 1)

            def squares(p, which, parity):
                act.wait_ge(s_unit, p * 4 + (U_QKV + which + 1))
                if not (isinstance(p, int) and p == 0):
                    act.wait_ge(s_st, p)
                nc.scalar.activation((sqq, sqk)[which], bank[which][:], ACT.Square).then_inc(s_qs, 1)
                if not (isinstance(p, int) and p == 0):
                    act.wait_ge(s_ql, p * 4 + (2 * which - 2))
                gain = gqs[:] if which == 0 else col(C_QK + 1)
                nc.scalar.activation((qg, kg)[which], bank[which][:], ACT.Copy,
                                     scale=gain).then_inc(s_qs, 1)

            def exponentials(head, h, pair):
                for n, (b, at, w) in enumerate(PACK):
                    act.wait_ge(s_neg, head * 4 + (n + 1))
                    nc.scalar.activation(sc[:, at:at + w], sc[:, at:at + w], ACT.Exp,
                                         bias=nmax[:, b:b + 1], scale=-1.0,
                                         accum_out=den[:, b:b + 1]).then_inc(s_e, 1)
                if not isinstance(pair, int) or pair < PAIRS - 1:
                    bias_load(h, pair + 1)

            def bias_load(h, pair):
                row = bias_rows[bass.ds(pair * 2 + h, 1), 0:1] if not isinstance(pair, int) else \
                    bias_rows[2 * pair + h:2 * pair + h + 1, 0:1]
                src = bass.AP(tensor=row.tensor, offset=row.offset, ap=[[1, P], [1, SEQ]])
                act.dma_start(toep[h], src).then_inc(s_t[h], 16)

            def round_pt(head):
                act.wait_ge(s_pt, head + 1)
                for at, end in ((0, SEQ), (SEQ, SCORES)):
                    nc.scalar.activation(pth[:, at:end], spt[:, at:end], ACT.Copy).then_inc(s_pth, 1)

            nc.scalar.activation(spare[:], gqs[:], ACT.Exp)
            act.wait_ge(s_rows, 16)
            for h in range(2):
                bias_load(h, 0)
            stage(0, 0, a=False, b=False)
            stage(1, 1, b=False)
            with act.Fori(1, PAIRS // 2) as i:
                stage(i * 2, 0)
                stage(i * 2 + 1, 1)
            stage(PAIRS, 0, qkv=False)
            stage(PAIRS + 1, 1, qkv=False, a=False)

            residual(3, U_WO)
            ffn(1, U_UP1, U_DOWN1)

        @block.vector
        def _(dve):
            steps = Steps(dve, s_small)
            link = steps.link

            def rsqrt(width, finish):
                v, half, t = (small[:, n, 0:width] for n in range(3))
                y = small[:, 4, 0:width]
                g = guess[:, 0:width]
                link(nc.vector.tensor_scalar(g, v.bitcast(I32), -0.5, MAGIC, ALU.mult, ALU.add))
                link(nc.vector.tensor_scalar(half, v, -0.5, None, ALU.mult))
                last = g.bitcast(F32)
                for n in range(3):
                    link(nc.vector.tensor_tensor(t, last, last, ALU.mult))
                    link(nc.vector.tensor_tensor(t, t, half, ALU.mult))
                    if n < 2:
                        link(nc.vector.scalar_tensor_tensor(y, t, 1.5, last, ALU.add, ALU.mult))
                    last = y
                finish(t, y)

            def clear_acc():
                nc.vector.memset(acc[:], 0.0).then_inc(s_acc, 1)

            def prep(norm, k):
                rest_x(norm, k)
                add_squares(norm, k, sq[:])

            def rest_x(norm, k):
                dve.wait_ge(s_xh, k + (norm * KT + 1))
                nc.vector.scalar_tensor_tensor(tile(xl, k), tile(x, k), col(k + (C_GAIN + norm * KT)),
                                               plain(tile(xh, k)), ALU.mult, ALU.subtract).then_inc(s_xl, 1)

            def add_squares(norm, k, squares):
                dve.wait_ge(s_sq, k + (norm * KT + 1))
                dve.wait_ge(s_acc, k + (norm * (KT + 1) + 1))
                nc.vector.tensor_tensor(acc[:], acc[:], squares, ALU.add).then_inc(s_acc, 1)

            def norm_rsqrt(norm):
                dve.wait_ge(s_ms, norm + 1)
                link(nc.vector.tensor_scalar(small[:, 0, 0:TB], nbank[:, 0:TB], EPS, None, ALU.add))
                if norm == 2:
                    link(nc.vector.tensor_scalar(epsv[:], small[:, 0, 0:TB], EPS, None, ALU.mult))
                rsqrt(TB, lambda t, y: nc.vector.scalar_tensor_tensor(
                    small[:, 3, 0:TB], t, 1.5, y, ALU.add, ALU.mult).then_inc(s_rn, 1))

            def rest_half(u):
                first = slice(0, SLOT // 2)
                nc.vector.tensor_tensor(wl[u][:, first], raw[u][:, first], plain(wh[u][:, first]),
                                        ALU.subtract).then_inc(s_lo_a, 1)

            link(nc.vector.memset(gate[:], 0.0))
            clear_acc()
            dve.wait_ge(s_par, 16)
            link(nc.vector.tensor_scalar(gqs[:], col(C_QK), HEAD ** -0.5, None, ALU.mult))
            rest_x(0, 0)
            dve.wait_ge(s_hi_a, 1)
            rest_half(0)
            for k in range(1, 4):
                rest_x(0, k)
            dve.wait_ge(s_hi, 2)
            rest_half(1)
            for k in range(4, KT):
                rest_x(0, k)
            dve.wait_ge(s_warm, 1)
            for k in range(KT):
                add_squares(0, k, sq_first[k % len(sq_first)])
            norm_rsqrt(0)

            dve.wait_ge(s_setup, 48)
            dve.wait_ge(s_bvmm, 2)
            heads = 2 * PAIRS
            link(nc.vector.tensor_tensor(bv_sb[0:heads, 0:SEQ], obank[0:heads, :],
                                         cnt_sb[0:heads, 0:SEQ], ALU.add))
            nc.vector.tensor_tensor(bv_sb[0:heads, SEQ:NVEC], rbank[0][0:heads, 0:NVEC - SEQ],
                                    cnt_sb[0:heads, SEQ:NVEC], ALU.add).then_inc(s_bv, 1)

            link(nc.vector.memset(zc[:, 0:2], 0.0))
            for buf in (pin, pa, pb):
                link(nc.vector.memset(buf[:, 0:PAD], 0.0))
            dve.wait_ge(s_pwh, 1)
            nc.vector.tensor_tensor(bl[:, POOLW, :], poolraw, plain(bh[:, POOLW, :]),
                                    ALU.subtract).then_inc(s_pwl, 1)
            dve.wait_ge(s_rstd, 1)
            for g in range(GROUPS):
                def scaled(dst, j):
                    dve.wait_ge(s_unit, U_IN + 4 * g + j + 1)
                    return nc.vector.tensor_tensor(dst, bank[j][:], rstd[:], ALU.mult)

                scaled(hs, 0).then_inc(s_inev, 1)
                scaled(cs, 1).then_inc(s_inev, 1)
                dve.wait_ge(s_inev, 4 * g + 2)
                nc.vector.tensor_tensor(zc[:, 2:], hs, cs, ALU.mult).then_inc(s_zc, 1)
                dve.wait_ge(s_cv, g + 1)
                for tap in (1, 0):
                    link(nc.vector.scalar_tensor_tensor(cv, zc[:, tap:tap + SEQ], col(C_CONVA + TAPS * g + tap),
                                                        cv, ALU.mult, ALU.add))
                scaled(cs, 2).then_inc(s_inev, 1)
                dve.wait_ge(s_inev, 4 * g + 3)
                nc.vector.tensor_tensor(ya, cs, cv, ALU.mult).then_inc(s_ya, 1)
                dve.wait_ge(s_yah, g + 1)
                nc.vector.tensor_tensor(bl[:, MIX + g, :], ya, plain(bh[:, MIX + g, :]),
                                        ALU.subtract).then_inc(s_yal, 1)
                scaled(pin[:, PAD:], 3).then_inc(s_inev, 1)
                dve.wait_ge(s_inev, 4 * g + 4)
                src, n = pin, 1
                for step in range(g + 1):
                    dst = (pa, pb)[step % 2]
                    link(nc.vector.tensor_tensor(dst[:, PAD:], src[:, PAD:], src[:, PAD - n:PAD - n + SEQ], ALU.add))
                    src, n = dst, 2 * n
                assert n == POOL_WINDOWS[g]
                link(nc.vector.scalar_tensor_tensor(pooled, src[:, PAD:], 1.0 / n, pin[:, PAD:],
                                                    ALU.mult, ALU.subtract))
                inv = par[:, C_INV + g * PAD:C_INV + (g + 1) * PAD]
                link(nc.vector.tensor_tensor(small[:, 0, :], src[:, PAD:2 * PAD], inv, ALU.mult))
                nc.vector.tensor_tensor(pooled[:, 0:PAD], small[:, 0, :], pin[:, PAD:2 * PAD],
                                        ALU.subtract).then_inc(s_pd, 1)
                dve.wait_ge(s_pdh, g + 1)
                nc.vector.tensor_tensor(bl[:, POOLED + g, :], pooled, plain(bh[:, POOLED + g, :]),
                                        ALU.subtract).then_inc(s_pdl, 1)
            for g in range(GROUPS):
                dve.wait_ge(s_ybh, g + 1)
                nc.vector.scalar_tensor_tensor(bl[:, MIX + GROUPS + g, :], bank[g][:], col(C_PSCALE + g),
                                               plain(bh[:, MIX + GROUPS + g, :]),
                                               ALU.mult, ALU.subtract).then_inc(s_ybl, 1)

            def add_residual(n, used, block_bank, done=s_unit):
                dve.wait_ge(done, used)
                nc.vector.tensor_tensor(tile(x, n), block_bank, tile(x, n), ALU.add).then_inc(s_x, 1)

            def start_norm(norm):
                dve.wait_ge(s_ms, norm)
                clear_acc()

            def residual(phase, base):
                start_norm(phase + 1)
                for n in range(KT):
                    early = phase == 2 and n < RING
                    if early and n == 0:
                        add_residual(n, 1, bank[n][:], s_wo0)
                    else:
                        add_residual(n, base + n + 1, bank[n][:] if early else rbank[n % 2])
                    if n:
                        prep(phase + 1, n - 1)
                prep(phase + 1, KT - 1)
                norm_rsqrt(phase + 1)

            def ffn(layer, up, down):
                for buf in zg + zu:
                    link(nc.vector.memset(buf[:, 0:2], 0.0))
                dve.wait_ge(s_rstd, 2 * layer + 2)

                def hidden(i, j, first=False):
                    f = i * 2 + (layer * FT + j)
                    c = C_FFN + layer * FT * 8 + j * 8
                    for n, buf in enumerate((zg[j], zu[j])):
                        dve.wait_ge(s_unit, i * 4 + (up + 2 * j + n + 1))
                        nc.vector.tensor_tensor(buf[:, 2:], bank[2 * j + n][:], rstd[:],
                                                ALU.mult).then_inc(s_z, 1)
                    if not first:
                        finish(f, 1 - j)
                    for tap, done, before in ((1, s_t1, s_id), (0, s_t0, s_t1)):
                        for n, (z, u) in enumerate(((zg[j], ug), (zu[j], uu[j]))):
                            dve.wait_ge(before, f * 2 + (n + 1))
                            nc.vector.scalar_tensor_tensor(
                                u, z[:, tap:tap + SEQ], col(i * 16 + (c + 4 * n + tap)), u,
                                ALU.mult, ALU.add).then_inc(done, 1)
                    if not first:
                        rest(f, i * 2 + (j - 1))

                def finish(f, j):
                    dve.wait_ge(s_silu, f)
                    dve.wait_ge(s_t0, f * 2)
                    if not isinstance(f, int) or f > 1:
                        dve.wait_ge(s_hl, f - 1)
                    nc.vector.tensor_tensor(hf, sg, uu[j], ALU.mult).then_inc(s_h, 1)

                def rest(f, k):
                    dve.wait_ge(s_hh, f)
                    nc.vector.tensor_tensor(tile(bl, k), hf, plain(tile(bh, k)), ALU.subtract).then_inc(s_hl, 1)

                hidden(0, 0, True)
                hidden(0, 1)
                with dve.Fori(1, FT // 2) as i:
                    hidden(i, 0)
                    hidden(i, 1)
                finish((layer + 1) * FT, 1)
                rest((layer + 1) * FT, FT - 1)

                if layer == 0:
                    start_norm(2)
                    add_residual(0, down + 4, rbank[0])
                    add_residual(1, down + 8, rbank[1])
                    prep(2, 0)
                    with dve.Fori(1, KT // 2) as i:
                        for j in range(2):
                            add_residual(i * 2 + j, i * 8 + (down + 4 * j + 4), rbank[j])
                            prep(2, i * 2 + (j - 1))
                    prep(2, KT - 1)
                    norm_rsqrt(2)
                else:
                    with dve.Fori(0, KT // 2) as i:
                        for j in range(2):
                            add_residual(i * 2 + j, i * 8 + (down + 4 * j + 4), rbank[j])

            residual(0, U_OUT)
            ffn(0, U_UP0, U_DOWN0)

            def scores(head, h, p):
                dve.wait_ge(s_t[h], p * 16)
                dve.wait_ge(s_s, head + 1)
                nc.vector.memset(gate[:], 0.0)
                for b, at, w in PACK:
                    u = w - 1
                    nc.vector.tensor_tensor_reduce(
                        sc[:, at:at + w], spt[:, at:at + w], toep[h][:, u::-1], -1.0, 3e38, ALU.add, ALU.min,
                        nmax[:, b:b + 1]).then_inc(s_neg, 1)

            def probabilities(head):
                dve.wait_ge(s_e, head * 4 + 4)
                link(nc.vector.reciprocal(rden[:], den[:]))
                for b, at, w in PACK:
                    nc.vector.tensor_scalar(sc[:, at:at + w], sc[:, at:at + w], rden[:, b:b + 1],
                                            None, ALU.mult).then_inc(s_p, 1)

            def rest_pt(head):
                for n, (at, end) in enumerate(((0, SEQ), (SEQ, SCORES))):
                    dve.wait_ge(s_pth, head * 2 + (n + 1))
                    nc.vector.tensor_tensor(ptl[:, at:end], spt[:, at:end], plain(pth[:, at:end]),
                                            ALU.subtract).then_inc(s_ptl, 1)

            def stage(p, parity, qkv=True, a=True, b=True):
                if b:
                    rest_pt((p - 2) * 2 + 1)
                    if not isinstance(p, int) or p <= PAIRS:
                        rest_output(p - 2, 0)
                if a:
                    scores((p - 1) * 2, 0, p)
                if b:
                    rest_output(p - 2, 1)
                if a:
                    probabilities((p - 1) * 2)
                    dve.wait_ge(s_vh, p)
                    nc.vector.tensor_tensor(v_heads(1 - parity, lo=True),
                                            mbank[:].rearrange("q (b h c) -> q b h c", b=TB, h=2),
                                            plain(v_heads(1 - parity, lo=False)), ALU.subtract).then_inc(s_vl, 1)
                    rest_pt((p - 1) * 2)
                if qkv:
                    dve.wait_ge(s_st, p + 1)
                    ms = small[:, 0, :].rearrange("q (w b h) -> q w b h", w=2, b=TB)
                    link(nc.vector.tensor_tensor(
                        ms, mbank[:, 0:16].rearrange("q (w b h) -> q w b h", w=2, b=TB),
                        spread(epsv[:], [[0, 2], [1, TB], [0, 2]]), ALU.add))
                    rsqrt(16, lambda t, y: widen(0))
                    widen(1)
                    normalise(p, 0, parity)
                if a:
                    scores((p - 1) * 2 + 1, 1, p)
                if qkv:
                    normalise(p, 1, parity)
                    for h in range(2):
                        dve.wait_ge(s_qh, p * 2 + (h + 1))
                        at = QT + 2 * parity + h
                        nc.vector.tensor_tensor(bh[half(1 - h), at, :], qg[half(h), :],
                                                plain(bh[half(h), at, :]), ALU.subtract).then_inc(s_ql, 1)
                if a:
                    probabilities((p - 1) * 2 + 1)
                if isinstance(p, int) and p == PAIRS:
                    rest_output(p - 1, 0)
                if qkv:
                    dve.wait_ge(s_unit, p * 4 + (U_QKV + 4))
                    if a:
                        dve.wait_ge(s_vt, p)
                    nc.vector.tensor_tensor(vf, bank[2][:], rstd[:], ALU.mult).then_inc(s_vf, 1)
                    for h in range(2):
                        dve.wait_ge(s_kh, p * 4 + (2 * h + 1))
                        nc.vector.tensor_tensor(bl[half(h), KREST + parity, :], kg[half(h), :],
                                                plain(bh[half(h), KTILE + 2 * parity + h, :]),
                                                ALU.subtract).then_inc(s_ql, 1)

            def rest_output(pair, h):
                rows = half(h)
                dve.wait_ge(s_oh, pair * 2 + (h + 1))
                if h or not isinstance(pair, int) or pair:
                    dve.wait_ge(s_ol, pair * 2 + h)
                nc.vector.tensor_tensor(left_over[rows, :], obank[rows, :],
                                        plain(tile(bh, pair + MIX)[rows, :]), ALU.subtract).then_inc(s_of, 1)
                dve.wait_ge(s_of, pair * 2 + (h + 1))
                nc.vector.tensor_tensor(tile(bl, pair + MIX)[rows, :], obank[half(1 - h), :],
                                        left_over[rows, :], ALU.add).then_inc(s_ol, 1)

            def widen(which):
                c = which * 2 * TB
                t, y = (spread(small[:, n, c:c + 1], [[1, 2 * TB], [0, HEAD]]) for n in (2, 4))
                wide = (rq, rk)[which].rearrange("q (c e) -> q c e", e=HEAD)
                nc.vector.scalar_tensor_tensor(wide, t, 1.5, y, ALU.add, ALU.mult).then_inc(s_r, 1)

            def normalise(p, which, parity):
                dve.wait_ge(s_rb, p * 2 + (which + 1))
                dve.wait_ge(s_qs, p * 4 + (2 * which + 2))
                buf = (qg, kg)[which]
                nc.vector.tensor_tensor(buf, mbank[:], buf, ALU.mult).then_inc(s_qn, 1)

            dve.wait_ge(s_rstd, 3)
            stage(0, 0, a=False, b=False)
            stage(1, 1, b=False)
            with dve.Fori(1, PAIRS // 2) as i:
                steps.loop(i, 1, 2 * (1 + 10 + 2))
                stage(i * 2, 0)
                stage(i * 2 + 1, 1)
            steps.end(PAIRS // 2 - 1)
            stage(PAIRS, 0, qkv=False)
            stage(PAIRS + 1, 1, qkv=False, a=False)

            residual(2, U_WO)
            ffn(1, U_UP1, U_DOWN1)

        @block.tensor
        def _(pe):
            mm = nc.tensor.matmul

            def product(dst, s, at, hi, lo, first, last):
                w = slice(at * P, (at + 1) * P)
                mm(dst, wh[s][:, w], hi, start=first, stop=False)
                mm(dst, wh[s][:, w], lo, start=False, stop=False)
                return mm(dst, wl[s][:, w], hi, start=False, stop=last)

            def unit_ready(u):
                pe.wait_ge(s_lo, u + 1)

            def project(dst, u, s, buf_h=xh, buf_l=xl, at=0):
                unit_ready(u)
                for k in range(KT):
                    last = product(dst, s, k, buf_h[:, at + k, :], buf_l[:, at + k, :], k == 0, k == KT - 1)
                last.then_inc(s_unit, 1)

            def norm_stats(norm):
                pe.wait_ge(s_acc, (norm + 1) * (KT + 1))
                for b in range(TB):
                    last = mm(nbank[:, b:b + 1], acc[:, b * P:(b + 1) * P], col(C_ONE), start=True, stop=True)
                last.then_inc(s_ms, 1)

            def norm_spread(norm):
                pe.wait_ge(s_rn, norm + 1)
                for b in range(TB):
                    r = spread(small[:, 3, b:b + 1], [[0, P]])
                    last = nc.tensor.transpose(nbank[:, b * P:(b + 1) * P], r, ident)
                last.then_inc(s_bc, 1)

            def first_two(norm, u):
                for k in range(KT):
                    pe.wait_ge(s_xl, norm * KT + k + 1)
                    if k == 4:
                        norm_stats(norm)
                    if k == KT - 1:
                        norm_spread(norm)
                    for n in range(2):
                        if k == 0:
                            unit_ready(u + n)
                        last = product(bank[n][:], n, k, xh[:, k, :], xl[:, k, :], k == 0, k == KT - 1)
                        if k == KT - 1:
                            last.then_inc(s_unit, 1)

            pe.wait_ge(s_acc, 1)
            for n in range(WARM):
                last = mm(obank[:], acc[:, 0:P], acc[:], start=True, stop=True)
            last.then_inc(s_warm, 1)

            def in_part(j, k0, k1):
                for k in range(k0, k1):
                    last = product(bank[j][:], j, k, xh[:, k, :], xl[:, k, :], k == 0, k == KT - 1)
                if k1 == KT:
                    last.then_inc(s_unit, 1)

            for n in range(2):
                pe.wait_ge(s_lo_a, n + 1)
                for k in range(KT // 2):
                    if n == 0:
                        pe.wait_ge(s_xl, k + 1)
                    in_part(n, k, k + 1)
            for n in range(2):
                unit_ready(U_IN + n)
                for k in range(KT // 2, KT):
                    if n == 0:
                        pe.wait_ge(s_xl, k + 1)
                    in_part(n, k, k + 1)
            unit_ready(U_IN + 2)
            in_part(2, 0, 5)
            pe.wait_ge(s_par_b, 16)
            norm_stats(0)
            in_part(2, 5, KT)
            pe.wait_ge(s_setup, 48)
            heads = 2 * PAIRS
            mm(obank[0:heads, :], rel_sb[0:BUCKETS, :], oh_sb[0:BUCKETS, 0:SEQ], start=True, stop=True).then_inc(s_bvmm, 1)
            mm(rbank[0][0:heads, 0:NVEC - SEQ], rel_sb[0:BUCKETS, :], oh_sb[0:BUCKETS, SEQ:NVEC],
               start=True, stop=True).then_inc(s_bvmm, 1)
            unit_ready(U_IN + 3)
            in_part(3, 0, 2)
            norm_spread(0)
            in_part(3, 2, KT)
            with pe.Fori(1, GROUPS) as i:
                for j in range(4):
                    pe.wait_ge(s_inev, i * 4 + (j - 3))
                    project(bank[j][:], i * 4 + (U_IN + j), j)
            pe.wait_ge(s_bv, 1)
            unit_ready(U_OUT)
            unit_ready(U_OUT + 1)

            def out_tile(k):
                for n in range(2):
                    last = product(rbank[n], n, k, bh[:, MIX + k, :], bl[:, MIX + k, :], k == 0, k == KT - 1)
                    if k == KT - 1:
                        last.then_inc(s_unit, 1)

            for g in range(GROUPS):
                pe.wait_ge(s_yal, g + 1)
                out_tile(g)
            pe.wait_ge(s_pwl, 1)
            for g in range(GROUPS):
                pe.wait_ge(s_pdl, g + 1)
                pe.wait_ge(s_inev, 4 * GROUPS - 3 + g)
                w = slice(g * P, (g + 1) * P)
                moving = (bh[:, POOLED + g, :], bl[:, POOLED + g, :])
                mm(bank[g][:], bh[:, POOLW, w], moving[0], start=True, stop=False)
                mm(bank[g][:], bh[:, POOLW, w], moving[1], start=False, stop=False)
                mm(bank[g][:], bl[:, POOLW, w], moving[0], start=False, stop=True).then_inc(s_yb, 1)
            for g in range(GROUPS):
                pe.wait_ge(s_ybl, g + 1)
                out_tile(GROUPS + g)

            def residual(phase, base, first=0):
                for n in range(first, KT):
                    if n >= RING + 2 or first == 2:
                        pe.wait_ge(s_x, phase * KT + n - 1)
                    project(rbank[n % 2], base + n, n % RING, bh, bl, MIX)

            residual(0, U_OUT, first=2)

            def ffn(layer, up, down):
                norm = 2 * layer + 1
                first_two(norm, up)
                for j in (2, 3):
                    project(bank[j][:], up + j, j)
                with pe.Fori(1, FT // 2) as i:
                    for j in range(4):
                        pe.wait_ge(s_z, i * 4 + (layer * 2 * FT + j - 3))
                        project(bank[j][:], i * 4 + (up + j), j)

                def down_block(i, j, first=False):
                    k = 0
                    for s, count_ in enumerate(DOWN_SPLIT):
                        unit_ready(i * 8 + (down + 4 * j + s))
                        if first:
                            pe.wait_ge(s_hl, layer * FT + k + count_)
                        for at in range(count_):
                            last = product(rbank[j], s, at, bh[:, k, :], bl[:, k, :], k == 0, k == FT - 1)
                            k += 1
                        last.then_inc(s_unit, 1)

                down_block(0, 0, True)
                down_block(0, 1)
                with pe.Fori(1, KT // 2) as i:
                    for j in range(2):
                        pe.wait_ge(s_x, i * 2 + (norm * KT + j - 1))
                        down_block(i, j)

            ffn(0, U_UP0, U_DOWN0)

            def qkv_part(p, which, s, k0, k1, at=0):
                for k in range(k0, k1):
                    last = product(bank[which][:], s, k - at, xh[:, k, :], xl[:, k, :], k == 0, k == KT - 1)
                return last

            def free_bank(p, which):
                if not (isinstance(p, int) and p == 0):
                    if which == 2:
                        pe.wait_ge(s_vf, p)
                    else:
                        pe.wait_ge(s_qs, p * 4 + (2 * which - 2))

            def score_blocks(head, h, parity, first=False):
                pe.wait_ge(s_ql, (head - h) * 2 + 4)
                pe.wait_ge(s_kh, (head - h) * 2 + 4)
                both, hi, rest_k = bh[:, QT + 2 * parity + h, :], bh[half(h), QT + 2 * parity + h, :], \
                    bl[half(h), KREST + parity, :]
                for n, (b, at, w) in enumerate(PACK):
                    if n < 2 and not first:
                        pe.wait_ge(s_ptl, head * 2 + (n - 1))
                    q = slice(b * P, (b + 1) * P)
                    mm(spt[:, at:at + w], both[:, q], bh[:, KTILE + 2 * parity + h, 0:w], start=True, stop=False)
                    last = mm(spt[:, at:at + w], hi[:, q], rest_k[:, 0:w], start=False, stop=True)
                last.then_inc(s_s, 1)

            def transposes(head):
                where = {b: at for b, at, _ in PACK}
                for n, (b, _, _) in enumerate(PACK):
                    pe.wait_ge(s_p, head * 4 + (n + 1))
                    for j in range(b + 1):
                        dst = where[TB - 1 - j]
                        last = nc.tensor.transpose(spt[:, dst + (b - j) * P:dst + (b - j + 1) * P],
                                                   sc[:, where[b] + j * P:where[b] + (j + 1) * P], ident)
                last.then_inc(s_pt, 1)

            def outputs(pair, h, parity):
                if h == 0:
                    pe.wait_ge(s_vl, pair + 1)
                if h or not isinstance(pair, int) or pair:
                    pe.wait_ge(s_ol, pair * 2 + h)
                where = {b: (at, w) for b, at, w in PACK}
                for j in range(TB):
                    if j < 2:
                        pe.wait_ge(s_ptl, pair * 4 + (2 * h + 1 + j))
                    at, w = where[TB - 1 - j]
                    at_v = j * VW + h * P
                    for n, pt in enumerate((pth, ptl)):
                        last = mm(obank[:, j * P:SEQ], v_tile(parity)[:, at_v:at_v + P], pt[:, at:at + w],
                                  start=j == 0 and n == 0, stop=j == TB - 1 and n == 1)
                last.then_inc(s_pv, 1)

            def stage(p, parity, qkv=True, a=True, b=True):
                begin = isinstance(p, int) and p == 0
                if begin:
                    first_two(2, U_QKV)
                elif qkv:
                    free_bank(p, 0)
                    unit_ready(p * 4 + U_QKV)
                    if b:
                        qkv_part(p, 0, 0, 0, 6)
                    else:
                        qkv_part(p, 0, 0, 0, 3)
                        spread_norm(0, 0)
                        qkv_part(p, 0, 0, 3, 6)
                        spread_norm(0, 1)
                if b:
                    transposes((p - 2) * 2 + 1)
                if qkv and not begin:
                    qkv_part(p, 0, 0, 6, KT).then_inc(s_unit, 1)
                    free_bank(p, 1)
                    unit_ready(p * 4 + (U_QKV + 1))
                    qkv_part(p, 1, 1, 0, 3 if b else 5)
                if a:
                    score_blocks((p - 1) * 2, 0, 1 - parity, first=not b)
                if b:
                    outputs(p - 2, 1, parity)
                if a:
                    turn_v(p - 1)
                if qkv and not begin:
                    qkv_part(p, 1, 1, 3 if b else 5, KT).then_inc(s_unit, 1)
                if qkv:
                    free_bank(p, 2)
                    unit_ready(p * 4 + (U_QKV + 2))
                    qkv_part(p, 2, 2, 0, 2)
                if a:
                    transposes((p - 1) * 2)
                if qkv:
                    qkv_part(p, 2, 2, 2, KT // 2).then_inc(s_unit, 1)
                    pe.wait_ge(s_qs, p * 4 + 3)
                    if a:
                        pe.wait_ge(s_vl, p)
                    for which, src in enumerate((sqq, sqk)):
                        for n in range(TB):
                            c = which * 2 * TB + 2 * n
                            last = mm(mbank[:, c:c + 2], src[:, n * P:(n + 1) * P],
                                      par[:, C_HEAD:C_HEAD + 2], start=True, stop=True)
                    last.then_inc(s_st, 1)
                if a:
                    score_blocks((p - 1) * 2 + 1, 1, 1 - parity)
                    outputs(p - 1, 0, 1 - parity)
                if qkv:
                    unit_ready(p * 4 + (U_QKV + 3))
                    qkv_part(p, 2, 3, 4, 5, at=KT // 2)
                    if not begin:
                        spread_norm(p, 0)
                    qkv_part(p, 2, 3, 5, 7, at=KT // 2)
                    if not begin:
                        spread_norm(p, 1)
                    qkv_part(p, 2, 3, 7, KT, at=KT // 2).then_inc(s_unit, 1)

            def turn_v(pair):
                pe.wait_ge(s_vf, pair + 1)
                pe.wait_ge(s_qn, pair * 2 + 2)
                for n in range(TB):
                    last = nc.tensor.transpose(mbank[:, n * P:(n + 1) * P], vf[:, n * P:(n + 1) * P], ident)
                last.then_inc(s_vt, 1)

            def spread_norm(p, which):
                pe.wait_ge(s_r, p * 2 + (which + 1))
                if which:
                    pe.wait_ge(s_qn, p * 2 + 1)
                for n in range(TB):
                    last = nc.tensor.transpose(mbank[:, n * P:(n + 1) * P],
                                               (rq, rk)[which][:, n * P:(n + 1) * P], ident)
                last.then_inc(s_rb, 1)

            stage(0, 0, a=False, b=False)
            stage(1, 1, b=False)
            with pe.Fori(1, PAIRS // 2) as i:
                stage(i * 2, 0)
                stage(i * 2 + 1, 1)
            def wo_part(n, k0, k1):
                if k0 == 0:
                    unit_ready(U_WO + n)
                for k in range(k0, k1):
                    pe.wait_ge(s_ol, 2 * k + 2)
                    last = product(bank[n][:], n, k, bh[:, MIX + k, :], bl[:, MIX + k, :], k == 0, k == KT - 1)
                if k1 == (KT if n else KT - 1):
                    last.then_inc(s_unit, 1)

            end = PAIRS - 1
            pe.wait_ge(s_qs, 4 * PAIRS)
            wo_part(0, 0, 5)
            transposes(2 * end - 1)
            wo_part(0, 5, 6)
            wo_part(1, 0, 3)
            score_blocks(2 * end, 0, 1)
            outputs(end - 1, 1, 0)
            turn_v(end)
            wo_part(1, 3, 6)
            wo_part(2, 0, 3)
            transposes(2 * end)
            wo_part(2, 3, 6)
            pe.wait_ge(s_kept, 2)
            wo_part(0, 6, 7)
            score_blocks(2 * end + 1, 1, 1)
            outputs(end, 0, 1)
            for n in (1, 2):
                wo_part(n, 6, 7)
            wo_part(3, 0, 5)
            transposes(2 * end + 1)
            wo_part(3, 5, 7)
            outputs(end, 1, 1)
            unit_ready(U_WO + RING)
            for k in range(5):
                product(rbank[0], 0, k, bh[:, MIX + k, :], bl[:, MIX + k, :], k == 0, False)
            pe.wait_ge(s_ol, 2 * KT)
            hi, lo = bh[:, MIX + KT - 1, :], bl[:, MIX + KT - 1, :]
            mm(bank[0][:], kept_h[:], hi, start=False, stop=False)
            mm(bank[0][:], kept_h[:], lo, start=False, stop=False)
            mm(bank[0][:], kept_l[:], hi, start=False, stop=True).then_inc(s_wo0, 1)
            for n in range(1, RING):
                wo_part(n, KT - 1, KT)
            for k in range(5, KT):
                last = product(rbank[0], 0, k, bh[:, MIX + k, :], bl[:, MIX + k, :], False, k == KT - 1)
            last.then_inc(s_unit, 1)
            residual(2, U_WO, first=RING + 1)
            ffn(1, U_UP1, U_DOWN1)


def column_tiles(w):
    k, n = w.shape
    return w.reshape(k // P, P, n // P, P).transpose(2, 1, 0, 3).reshape(n // P, P, k)


def pack_params(even_norm, odd_norm, ffn_norm, q_norm, k_norm, conv_a, pool_scale, ffn_w, ffn_b):
    out = np.zeros((P, NPAR), np.float32)
    for n, g in enumerate((even_norm[0], ffn_norm[0], odd_norm[0], ffn_norm[1])):
        out[:, C_GAIN + n * KT:C_GAIN + (n + 1) * KT] = g.reshape(KT, P).T
    out[:, C_QK] = np.concatenate([q_norm[0]] * 2)
    out[:, C_QK + 1] = np.concatenate([k_norm[0]] * 2)
    out[:, C_CONVA:C_PSCALE] = conv_a[0].reshape(TAPS, GROUPS, P).transpose(2, 1, 0).reshape(P, -1)
    out[:, C_PSCALE:C_FFN] = pool_scale[0].reshape(GROUPS, P).T
    taps = np.concatenate([ffn_w, ffn_b[:, None]], axis=1)
    taps = taps.reshape(2, TAPS + 1, 2, FT, P).transpose(4, 0, 3, 2, 1)
    out[:, C_FFN:C_ONE] = taps.reshape(P, -1)
    out[:, C_ONE] = 1.0 / D
    out[:HEAD, C_HEAD] = 1.0 / HEAD
    out[HEAD:, C_HEAD + 1] = 1.0 / HEAD
    for g, n in enumerate(POOL_WINDOWS):
        out[:, C_INV + g * PAD:C_INV + (g + 1) * PAD] = 1.0 / np.minimum(np.arange(1, PAD + 1), n)
    out[:, C_IDENT:] = np.eye(P, dtype=np.float32)
    return out


def build(nc, shapes):
    ins = [nc.dram_tensor(name, shape, F32, kind="ExternalInput").ap() for name, shape in shapes.items()]
    out = nc.dram_tensor("out_t", [KT, P, SEQ], F32, kind="ExternalOutput").ap()
    trunk(nc, *ins, out)


def kernel(x, rel_bias, even_norm, even_w_in, even_conv_w, even_pool_w, even_pool_scale, even_w_out,
           odd_norm, odd_w_qkv, odd_q_norm, odd_k_norm, odd_w_o, ffn_norm, ffn_w_up, ffn_conv_w,
           ffn_conv_b, ffn_w_down):
    import concourse.bacc as bacc
    from concourse.bass_utils import run_bass_kernel_spmd

    onehot, count = shape_constants()
    a = np.asarray
    tiles_in = column_tiles(a(even_w_in)[0]).reshape(4, GROUPS, P, D)
    up = np.stack([column_tiles(w) for w in a(ffn_w_up)])
    qkv = column_tiles(a(odd_w_qkv)[0]).reshape(3, PAIRS, P, D)
    arrays = {
        "xt": a(x)[0].T.reshape(KT, P, SEQ).transpose(1, 0, 2),
        "params": pack_params(a(even_norm), a(odd_norm), a(ffn_norm), a(odd_q_norm), a(odd_k_norm),
                              a(even_conv_w), a(even_pool_scale), a(ffn_conv_w), a(ffn_conv_b)),
        "onehot": onehot,
        "count": count,
        "rel": a(rel_bias),
        "poolw": a(even_pool_w)[0].transpose(1, 0, 2).reshape(P, GROUPS * P),
        "w_in": tiles_in[[0, 2, 1, 3]].transpose(1, 0, 2, 3).reshape(4 * GROUPS, P, D),
        "w_out": column_tiles(a(even_w_out)[0]),
        "w_up": up.reshape(2, 2, FT, P, D).transpose(0, 2, 1, 3, 4).reshape(4 * FT, P, D),
        "w_down": np.concatenate([column_tiles(w) for w in a(ffn_w_down)]),
        "w_qkv": qkv.transpose(1, 2, 0, 3).reshape(PAIRS, P, 3 * D),
        "w_o": column_tiles(a(odd_w_o)[0]),
    }
    arrays = {name: np.ascontiguousarray(v) for name, v in arrays.items()}
    nc = bacc.Bacc("TRN2", target_bir_lowering=False, num_devices=1, dynamic_dma_scratch_size=1024)
    build(nc, {name: list(v.shape) for name, v in arrays.items()})
    result = run_bass_kernel_spmd(nc, [arrays], core_ids=[0])
    got = result.results[0]["out_t"]
    return np.ascontiguousarray(got.reshape(D, SEQ).T)[None]
```
